# Optimizing a Trainium2 kernel written in Bass

```python
import jax, jax.numpy as jnp
from jax import lax
import numpy as np

D_MODEL = 2048
BATCH = 1
SEQ = 256
DEPTH = 1

CHUNK = 64
D_MIX = D_MODEL
GMLP_HEADS = 8
GMLP_HEAD_DIM = 128
GMLP_WIDTH = GMLP_HEADS * GMLP_HEAD_DIM
GMLP_BLOCK = 128
MLA_HEADS = 8
MLA_NOPE = 128
MLA_ROPE = 64
MLA_QK = MLA_NOPE + MLA_ROPE
MLA_V = 128
MLA_WIDTH = MLA_HEADS * MLA_V
MLA_Q_RANK = 512
MLA_KV_RANK = 256
ROPE_THETA = 10000.0
Q_BLOCK = 128
PEER_HEADS = 8
PEER_N_KEYS = 128
PEER_N_EXPERTS = PEER_N_KEYS * PEER_N_KEYS
PEER_D_KEY = 256
PEER_D_HALF = PEER_D_KEY // 2
PEER_TOPK = 16
PEER_TOKEN_BLOCK = 128
RMS_EPS = 1e-6
IN_COLS = 2 * GMLP_WIDTH + MLA_Q_RANK + MLA_KV_RANK + MLA_ROPE
SPLIT_POINTS = (2 * GMLP_WIDTH, 2 * GMLP_WIDTH + MLA_Q_RANK, 2 * GMLP_WIDTH + MLA_Q_RANK + MLA_KV_RANK)

kernel_name = "hybrid_gmlp_mla_peer_block"

def rmsnorm(x, g):
    xf = x.astype(jnp.float32)
    xf = xf * lax.rsqrt(jnp.mean(xf * xf, axis=-1, keepdims=True) + RMS_EPS)
    return xf.astype(x.dtype) * g

def rope_tables(seq_len, dtype):
    pos = jnp.arange(seq_len, dtype=jnp.float32)
    inv_freq = ROPE_THETA ** (-jnp.arange(0, MLA_ROPE, 2, dtype=jnp.float32) / MLA_ROPE)
    ang = pos[:, None] * inv_freq[None, :]
    return jnp.cos(ang).astype(dtype), jnp.sin(ang).astype(dtype)

def apply_rope(x, cos, sin):
    c = cos[None, :, None, :]
    s = sin[None, :, None, :]
    x1, x2 = jnp.split(x, 2, axis=-1)
    return jnp.concatenate([x1 * c - x2 * s, x1 * s + x2 * c], axis=-1)

def gmlp_mixer(z, vnorm_g, ws, bs):
    bsz, seq, _ = z.shape
    z = jax.nn.gelu(z)
    u, v = jnp.split(z, 2, axis=-1)
    v = rmsnorm(v, vnorm_g)
    nblk = seq // GMLP_BLOCK
    v = v.reshape(bsz, nblk, GMLP_BLOCK, GMLP_HEADS, GMLP_HEAD_DIM)
    mask = jnp.tril(jnp.ones((GMLP_BLOCK, GMLP_BLOCK), dtype=bool))
    w = jnp.where(mask[None], ws, jnp.zeros_like(ws))
    sv = jnp.einsum('hij,bnjhc->bnihc', w, v) + bs.T[None, None, :, :, None]
    return u * sv.reshape(bsz, seq, GMLP_WIDTH)

def mla_mixer(c_q, c_kv, k_rope, qnorm_g, w_uq, kvnorm_g, w_ukv, qk_q_g, qk_k_g, cos, sin):
    bsz, seq, _ = c_q.shape
    q = (rmsnorm(c_q, qnorm_g) @ w_uq).reshape(bsz, seq, MLA_HEADS, MLA_QK)
    kv = (rmsnorm(c_kv, kvnorm_g) @ w_ukv).reshape(bsz, seq, MLA_HEADS, MLA_NOPE + MLA_V)
    k_nope, v = kv[..., :MLA_NOPE], kv[..., MLA_NOPE:]
    k_r = jnp.broadcast_to(k_rope[:, :, None, :], (bsz, seq, MLA_HEADS, MLA_ROPE))
    k = jnp.concatenate([k_nope, k_r], axis=-1)
    q = rmsnorm(q, qk_q_g)
    k = rmsnorm(k, qk_k_g)
    q = jnp.concatenate([q[..., :MLA_NOPE], apply_rope(q[..., MLA_NOPE:], cos, sin)], axis=-1)
    k = jnp.concatenate([k[..., :MLA_NOPE], apply_rope(k[..., MLA_NOPE:], cos, sin)], axis=-1)
    q = q * (MLA_QK ** -0.5)
    key_chunk = jnp.arange(seq) // CHUNK

    def attend_block(i):
        start = i * Q_BLOCK
        qb = lax.dynamic_slice_in_dim(q, start, Q_BLOCK, axis=1)
        s = jnp.einsum('bqhd,bkhd->bhqk', qb, k).astype(jnp.float32)
        q_chunk = (start + jnp.arange(Q_BLOCK)) // CHUNK
        allowed = key_chunk[None, :] <= q_chunk[:, None]
        s = jnp.where(allowed[None, None], s, -jnp.inf)
        p = jax.nn.softmax(s, axis=-1).astype(v.dtype)
        return jnp.einsum('bhqk,bkhd->bqhd', p, v)

    out = lax.map(attend_block, jnp.arange(seq // Q_BLOCK))
    return out.transpose(1, 0, 2, 3, 4).reshape(bsz, seq, MLA_WIDTH)

def peer_ffn(x, w_q, subkeys, u_tab, v_tab):
    bsz, seq, d = x.shape
    xb = x.reshape(bsz * seq // PEER_TOKEN_BLOCK, PEER_TOKEN_BLOCK, d)

    def retrieve(xblk):
        t = xblk.shape[0]
        q = (xblk @ w_q).reshape(t, PEER_HEADS, 2, PEER_D_HALF)
        s = jnp.einsum('thpd,hpnd->thpn', q, subkeys).astype(jnp.float32)
        sv, si = lax.top_k(s, PEER_TOPK)
        cand = (sv[:, :, 0, :, None] + sv[:, :, 1, None, :]).reshape(t, PEER_HEADS, PEER_TOPK * PEER_TOPK)
        cand_id = (si[:, :, 0, :, None] * PEER_N_KEYS + si[:, :, 1, None, :]).reshape(t, PEER_HEADS, PEER_TOPK * PEER_TOPK)
        top_s, top_pos = lax.top_k(cand, PEER_TOPK)
        experts = jnp.take_along_axis(cand_id, top_pos, axis=-1)
        g = jax.nn.softmax(top_s, axis=-1).astype(xblk.dtype)
        u = u_tab[experts]
        a = jax.nn.gelu(jnp.einsum('thkd,td->thk', u, xblk))
        vv = v_tab[experts]
        return jnp.einsum('thk,thkd->td', g * a, vv)

    return lax.map(retrieve, xb).reshape(bsz, seq, d)

def setup_inputs(seed: int = 0) -> dict:
    key = jax.random.key(seed)
    ks = jax.random.split(key, 18)
    f32 = jnp.float32
    nrm = lambda k, shape, scale: jax.random.normal(k, shape, f32) * scale
    gain = lambda k, n: 1.0 + 0.05 * jax.random.normal(k, (DEPTH, n), f32)
    return {
        "x": nrm(ks[0], (BATCH, SEQ, D_MODEL), 1.0),
        "norm_mix_g": gain(ks[1], D_MODEL),
        "w_in": nrm(ks[2], (DEPTH, D_MODEL, IN_COLS), D_MODEL ** -0.5),
        "gmlp_vnorm_g": gain(ks[3], GMLP_WIDTH),
        "gmlp_ws": nrm(ks[4], (DEPTH, GMLP_HEADS, GMLP_BLOCK, GMLP_BLOCK), GMLP_BLOCK ** -0.5),
        "gmlp_bs": 1.0 + nrm(ks[5], (DEPTH, GMLP_HEADS, GMLP_BLOCK), 0.1),
        "mla_qnorm_g": gain(ks[6], MLA_Q_RANK),
        "mla_w_uq": nrm(ks[7], (DEPTH, MLA_Q_RANK, MLA_HEADS * MLA_QK), MLA_Q_RANK ** -0.5),
        "mla_kvnorm_g": gain(ks[8], MLA_KV_RANK),
        "mla_w_ukv": nrm(ks[9], (DEPTH, MLA_KV_RANK, MLA_HEADS * (MLA_NOPE + MLA_V)), MLA_KV_RANK ** -0.5),
        "mla_qk_q_g": gain(ks[10], MLA_QK),
        "mla_qk_k_g": gain(ks[11], MLA_QK),
        "w_out": nrm(ks[12], (DEPTH, D_MIX, D_MODEL), D_MIX ** -0.5),
        "norm_ffn_g": gain(ks[13], D_MODEL),
        "peer_w_q": nrm(ks[14], (DEPTH, D_MODEL, PEER_HEADS * PEER_D_KEY), D_MODEL ** -0.5),
        "peer_subkeys": nrm(ks[15], (DEPTH, PEER_HEADS, 2, PEER_N_KEYS, PEER_D_HALF), PEER_D_HALF ** -0.5),
        "peer_u": nrm(ks[16], (DEPTH, PEER_N_EXPERTS, D_MODEL), D_MODEL ** -0.5),
        "peer_v": nrm(ks[17], (DEPTH, PEER_N_EXPERTS, D_MODEL), PEER_HEADS ** -0.5),
    }

def reference(x, norm_mix_g, w_in, gmlp_vnorm_g, gmlp_ws, gmlp_bs, mla_qnorm_g, mla_w_uq,
              mla_kvnorm_g, mla_w_ukv, mla_qk_q_g, mla_qk_k_g, w_out, norm_ffn_g,
              peer_w_q, peer_subkeys, peer_u, peer_v):
    cos, sin = rope_tables(x.shape[1], x.dtype)
    for l in range(DEPTH):
        h = rmsnorm(x, norm_mix_g[l])
        proj = h @ w_in[l]
        z_a, c_q, c_kv, k_rope = jnp.split(proj, SPLIT_POINTS, axis=-1)
        out_a = gmlp_mixer(z_a, gmlp_vnorm_g[l], gmlp_ws[l], gmlp_bs[l])
        out_b = mla_mixer(c_q, c_kv, k_rope, mla_qnorm_g[l], mla_w_uq[l], mla_kvnorm_g[l],
                          mla_w_ukv[l], mla_qk_q_g[l], mla_qk_k_g[l], cos, sin)
        x = x + jnp.concatenate([out_a, out_b], axis=-1) @ w_out[l]
        x = x + peer_ffn(rmsnorm(x, norm_ffn_g[l]), peer_w_q[l], peer_subkeys[l], peer_u[l], peer_v[l])
    return x


_drawn_inputs = setup_inputs


def setup_inputs(seed=0):
    import zlib

    import numpy as np

    out = dict(_drawn_inputs(seed))
    spreads = {}
    factors = {'mla_qnorm_g': 4.453,
     'mla_kvnorm_g': 4.081,
     'mla_qk_q_g': 4.693,
     'mla_qk_k_g': 4.761,
     'gmlp_vnorm_g': 8.0,
     'gmlp_bs': 3.117,
     'norm_ffn_g': 3.927}
    for name, (base, spread) in spreads.items():
        noise = np.random.default_rng([zlib.crc32(name.encode()), seed]).standard_normal(out[name].shape)
        drawn = base * np.exp(spread * noise) if base else spread * noise
        out[name] = __import__('jax').numpy.asarray(drawn.astype(out[name].dtype))
    for name, factor in factors.items():
        out[name] = (out[name] * factor).astype(out[name].dtype)
    return out
```

```python
from contextlib import ExitStack

import concourse.bass as bass
from concourse import mybir

F32 = mybir.dt.float32
F32R = mybir.dt.float32r
U32 = mybir.dt.uint32
ALU = mybir.AluOpType
ACT = mybir.ActivationFunctionType
AX = mybir.AxisListType

P = 128
SEQ = 256
D = 2048
NB = SEQ // P
KD = D // P
HEADS = 8
NOPE, ROPE, QK = 128, 64, 192
Q_RANK, KV_RANK = 512, 256
LAT = Q_RANK + KV_RANK + ROPE
GW = 1024
CHUNK = 64
NKEYS = 128
TOPK = 16
HP = 16
EPS = 1e-6
QSCALE = float(QK) ** -0.5
NEG = -1.0e30
LOWEST = -3.0e38

PIECE = 1024
RAW = 4
SPL = 2
COLG = 512

KP = 2
GROUPS = []


def _groups():
    n = 0
    for what, pieces, cols in (
        [("cq", 8, Q_RANK), ("ckv", 8, KV_RANK + ROPE), ("zv", 8, COLG)] + [("q", 2, COLG)] * 3
        + [("kv", 1, COLG)] * 4 + [("zv", 8, COLG)] + [("zu", 8, COLG)] * 2 + [("out", 8, COLG)] * 4
    ):
        GROUPS.append((what, n, pieces, cols))
        n += pieces
    return n


WQ0 = _groups()
U0 = WQ0 + 2 * HP
V0 = U0 + 2 * NKEYS
X0 = V0 + 2 * NKEYS
FIRST_OUT = GROUPS[13][1]

C_MIX, C_FFN, C_QN, C_KVN, C_QG, C_KG, C_BS = 0, 16, 32, 36, 38, 39, 40
NCOLS = 48
R_V, R_Q, R_K = 0, GW, GW + ROPE
NROWS = GW + 2 * ROPE


def build(nc, d, out):
    ctx = ExitStack()
    front_ctx = ExitStack()

    def sb(name, shape, dt=F32, c=ctx):
        return c.enter_context(nc.sbuf_tensor(name, shape, dt))

    def sem(name):
        return ctx.enter_context(nc.semaphore(name))

    with ctx:
        raw = sb("raw", [P, RAW, PIECE])
        hi = sb("hi", [P, SPL, PIECE], F32R)
        lo = sb("lo", [P, SPL, PIECE], F32R)
        ht_hi = sb("ht_hi", [P, KD, SEQ], F32R)
        ht_lo = sb("ht_lo", [P, KD, SEQ], F32R)
        ident = sb("ident", [P, P])
        iota = sb("iota", [P, P])
        cols = sb("cols", [P, NCOLS])
        rows = sb("rows", [P, NROWS])
        rope = sb("rope", [P, NB, 2, ROPE // 2])
        wst = sb("wst", [P, HEADS, P])
        st = sb("st", [P, 64])
        rs = sb("rs", [P, 64])
        rr = sb("rr", [P, 64])
        nmax = sb("nmax", [P, 2, NB, HEADS])
        sums = sb("sums", [P, 2, NB, HEADS])
        gq = sb("gq", [P, 1])
        mrow = sb("mrow", [P, P + SEQ])
        picks = sb("picks", [P, 3, SEQ])
        one_i = sb("one_i", [P, 2, 4, P])
        one_j = sb("one_j", [P, 2, 4, P])
        c_hi = sb("c_hi", [P, 2, SEQ], F32R)
        c_lo = sb("c_lo", [P, 2, SEQ], F32R)
        bank = [ctx.enter_context(nc.psum_tensor(f"bank{i}", [P, COLG], F32)) for i in range(8)]

        FRONT = 24192 + NB * HEADS * ROPE
        front = sb("front", [P, FRONT], F32, front_ctx)
        mix_hi = sb("mix_hi", [P, HEADS, SEQ], F32R, front_ctx)
        mix_lo = sb("mix_lo", [P, HEADS, SEQ], F32R, front_ctx)
        ct_hi = sb("ct_hi", [P, 6, SEQ], F32R, front_ctx)
        ct_lo = sb("ct_lo", [P, 6, SEQ], F32R, front_ctx)
        front_ctx.close()
        act_all = sb("act_all", [P, NKEYS, SEQ])

        at = [0]

        def cut(*shape):
            n = 1
            for s in shape:
                n *= s
            v = front[:, at[0]:at[0] + n]
            at[0] += n
            names = "abcd"[:len(shape)]
            return v.rearrange(f"p ({' '.join(names)}) -> p {' '.join(names)}",
                               **dict(zip(names[1:], shape[1:])))

        qt = cut(HEADS, SEQ)
        qtr = cut(HEADS // 2, SEQ)
        kt = cut(HEADS, SEQ)
        ktr = cut(HEADS // 2, SEQ)
        squares = front[:, 0:at[0]]
        kv = cut(NB, HEADS, 2 * NOPE)
        z0 = at[0]
        zv = cut(NB, GW)
        zu = cut(NB, GW)
        xs = front[:, z0:z0 + NB * D].rearrange("p (b n) -> p b n", b=NB)
        q0 = at[0]
        q = cut(NB, HEADS, QK)
        kr = cut(NB, HEADS, ROPE)
        lat = cut(NB, LAT)
        prob = front[:, q0:q0 + HEADS * SEQ].rearrange("p (h n) -> p h n", h=HEADS)
        prt = front[:, q0 + HEADS * SEQ:q0 + 2 * HEADS * SEQ].rearrange("p (h k n) -> p h k n", h=HEADS, k=2)
        x = cut(NB, D)
        qr = cut(NB, HEADS, ROPE)
        assert at[0] == FRONT
        sq_x = squares[:, 0:NB * D].rearrange("p (b n) -> p b n", b=NB)
        sq_q = squares[:, 0:NB * HEADS * QK].rearrange("p (b h n) -> p b h n", b=NB, h=HEADS)
        sq_k = squares[:, NB * HEADS * QK:NB * HEADS * (QK + NOPE)].rearrange("p (b h n) -> p b h n", b=NB, h=HEADS)
        tmp_q = squares[:, 0:HEADS * QK]
        tmp_k = squares[:, HEADS * QK:2 * HEADS * QK]

        LAST_FREE = 96
        flat = act_all[:, LAST_FREE:NKEYS, :].rearrange("p j t -> p (j t)")
        NTOP = NB * HEADS * TOPK
        sat = [0]

        def scratch(n):
            v = flat[:, sat[0]:sat[0] + n]
            sat[0] += n
            return v

        keys_at = scratch(HP * NKEYS)
        subkeys = keys_at.rearrange("p (h n) -> p h n", h=HP)
        score = scratch(NB * HP * NKEYS)
        qp_at = scratch(2 * SEQ)
        qp = qp_at.rearrange("p (c n) -> p c n", c=2)
        sw = scratch(2 * NKEYS).rearrange("p (a n) -> p a n", a=2)
        sw2 = scratch(NKEYS)
        cand = scratch(TOPK * TOPK)
        cand2 = scratch(TOPK * TOPK)
        sv = scratch(2 * TOPK)
        tops = scratch(TOPK)
        i8 = scratch(2 * TOPK).bitcast(U32)
        pos = scratch(TOPK).bitcast(U32)
        assert sat[0] <= (NKEYS - LAST_FREE) * SEQ
        all_top = keys_at[:, 0:NTOP]
        all_pos = keys_at[:, NTOP:2 * NTOP].bitcast(U32)
        all_id = keys_at[:, 2 * NTOP:4 * NTOP].bitcast(U32)
        idf = keys_at[:, 4 * NTOP:6 * NTOP]
        posu = keys_at[:, 6 * NTOP:8 * NTOP].bitcast(U32)
        posf = qp_at[:, 0:2 * NTOP]
        hot = score[:, 0:1024]
        key_of = score[:, 1024:1024 + 2 * NTOP]
        gate = score[:, 1536:1536 + NTOP]
        smx = score[:, 1792:1792 + 2 * NB * HEADS]

        S_X, S_LAT, S_Q, S_K, S_V, S_X2, S_PART, S_KR = 0, 2, 6, 22, 38, 40, 42, 50

        cols_in = sem("cols_in")
        rows_in = sem("rows_in")
        wst_in = sem("wst_in")
        x_in = sem("x_in")
        sub_in = sem("sub_in")
        x2_out = sem("x2_out")
        raw_in = [sem(f"raw_in{i}") for i in range(RAW)]
        hi_done = sem("hi_done")
        lo_done = sem("lo_done")
        used = sem("used")
        ident_set = sem("ident_set")
        iota_set = sem("iota_set")
        mask_set = sem("mask_set")
        wst_masked = sem("wst_masked")
        turned = sem("turned")
        t_hi = sem("t_hi")
        t_lo = sem("t_lo")
        acc_out = sem("acc_out")
        stat = sem("stat")
        root = sem("root")
        scaled = sem("scaled")
        sq_done = sem("sq_done")
        q_ready = sem("q_ready")
        k_norm = sem("k_norm")
        k_ready = sem("k_ready")
        gq_set = sem("gq_set")
        qk_turned = sem("qk_turned")
        qk_out = sem("qk_out")
        s_ready = sem("s_ready")
        s_max = sem("s_max")
        s_exp = sem("s_exp")
        p_ready = sem("p_ready")
        p_turned = sem("p_turned")
        p_out = sem("p_out")
        pv_ready = sem("pv_ready")
        pv_hi = sem("pv_hi")
        pv_lo = sem("pv_lo")
        v_ready = sem("v_ready")
        sv_ready = sem("sv_ready")
        gm_ready = sem("gm_ready")
        x2_ready = sem("x2_ready")
        x2_sq = sem("x2_sq")
        q_out = sem("q_out")
        sc_ready = sem("sc_ready")
        sc_out = sem("sc_out")
        a_out = sem("a_out")
        gate_in = sem("gate_in")
        gate_exp = sem("gate_exp")
        picks_ready = sem("picks_ready")
        picks_turned = sem("picks_turned")
        picks_out = sem("picks_out")
        hot_ready = sem("hot_ready")
        g_ready = sem("g_ready")
        g_used = sem("g_used")
        ch_done = sem("ch_done")
        cl_done = sem("cl_done")
        y_ready = sem("y_ready")
        y_sent = sem("y_sent")
        dve_step = sem("dve_step")
        dve_topk = sem("dve_topk")
        dve_pick = sem("dve_pick")
        dve_late = sem("dve_late")
        pool_step = sem("pool_step")

        x_rows = d["x"].rearrange("(b p) n -> p b n", p=P)
        x2_rows = d["x2"].rearrange("(b p) n -> p b n", p=P)
        out_rows = out.rearrange("(b p) n -> p b n", p=P)

        def group_of(n):
            for g, (what, first, pieces, c) in enumerate(GROUPS):
                if first <= n < first + pieces:
                    return g, what, n - first, pieces, c

        def linked(eng, s, base=0):
            count = [0]

            def link(ins):
                count[0] += 1
                ins.then_inc(s, 1)
                eng.wait_ge(s, base + count[0])
            return link

        def bc(v, n):
            return v.unsqueeze(2).to_broadcast((v.shape[0], v.shape[1], n))

        def over_heads(v):
            return v.unsqueeze(1).to_broadcast((P, HEADS, v.shape[1]))

        def rotate(e, link, v, b, tmp, done):
            h = ROPE // 2
            cos, sin = over_heads(rope[:, b, 0, :]), over_heads(rope[:, b, 1, :])
            t = [tmp[:, k * HEADS * h:(k + 1) * HEADS * h].rearrange("p (h n) -> p h n", h=HEADS) for k in range(4)]
            link(e.tensor_tensor(t[0], v[:, :, 0:h], cos, ALU.mult))
            link(e.tensor_tensor(t[1], v[:, :, h:2 * h], sin, ALU.mult))
            link(e.tensor_tensor(t[2], v[:, :, 0:h], sin, ALU.mult))
            link(e.tensor_tensor(t[3], v[:, :, h:2 * h], cos, ALU.mult))
            link(e.tensor_tensor(v[:, :, 0:h], t[0], t[1], ALU.subtract))
            e.tensor_tensor(v[:, :, h:2 * h], t[2], t[3], ALU.add).then_inc(done, 1)

        splits = [
            (lambda k, b: xs[:, b, k * P:(k + 1) * P], C_MIX, ht_hi, ht_lo, KD),
            (lambda k, b: lat[:, b, k * P:(k + 1) * P], C_QN, ct_hi, ct_lo, 6),
            (lambda k, b: zu[:, b, k * P:(k + 1) * P], None, ht_hi, ht_lo, HEADS),
            (lambda k, b: xs[:, b, k * P:(k + 1) * P], C_FFN, ht_hi, ht_lo, KD),
        ]
        fills_before = [0]
        for s in splits:
            fills_before.append(fills_before[-1] + s[4] // 2)

        def gain_of(s, k):
            gain = splits[s][1]
            return 1.0 if gain is None else cols[:, gain + k:gain + k + 1]

        block = ctx.enter_context(nc.Block())

        @block.sync
        def _(sp):
            sp.dma_start(x[:, 0, :], x_rows[:, 0, :]).then_inc(x_in, 16)
            sp.dma_start(x[:, 1, :], x_rows[:, 1, :]).then_inc(x_in, 16)
            sp.dma_start(cols[:, :], d["cols"]).then_inc(cols_in, 16)

            def load(n, i, src, width=PIECE):
                if n >= RAW:
                    sp.wait_ge(lo_done, i * 4 + (n - RAW + 1))
                sp.dma_start(raw[:, n % RAW, 0:width], src).then_inc(raw_in[n % RAW], 16)

            seen = {}
            for n in range(WQ0):
                g, what, k, pieces, c = group_of(n)
                m = seen.get(what, 0)
                seen[what] = m + 1
                load(n, 0, d["w_uq" if what == "q" else "w_" + what][m], KP * c)
                if n == RAW - 1:
                    sp.dma_start(rows[:, :], d["rows"].to_broadcast((P, NROWS))).then_inc(rows_in, 16)
                    sp.dma_start(rope[:, :, :, :], d["rope"]).then_inc(rows_in, 16)
                    sp.dma_start(wst[:, :, :], d["ws"]).then_inc(wst_in, 16)
            for p in range(4):
                load(WQ0 + p, 0, d["w_pq"][p])
            sp.wait_ge(used, WQ0)
            sp.dma_start(subkeys, d["subkeys"]).then_inc(sub_in, 16)

            def four(first, i, src):
                for p in range(4):
                    load(first + p, i, src[bass.ds(i * 4 + p, 1)].rearrange("a p n -> (a p) n"))

            with sp.Fori(1, HP // 2) as i:
                four(WQ0, i, d["w_pq"])
            with sp.Fori(0, NKEYS // 2) as i:
                four(U0, i, d["peer_u"])
            with sp.Fori(0, NKEYS // 2) as i:
                four(V0, i, d["peer_v"])
            sp.wait_ge(x2_out, 16)
            for p in range(4):
                load(X0 + p, 0, x2_rows[:, p // 2, (p % 2) * PIECE:(p % 2 + 1) * PIECE])
            for p in range(4):
                sp.wait_ge(y_ready, p + 1)
                sp.dma_start(out_rows[:, p // 2, (p % 2) * PIECE:(p % 2 + 1) * PIECE],
                             raw[:, (X0 + p) % RAW, :]).then_inc(y_sent, 16)
            sp.wait_ge(y_sent, 64)

        @block.gpsimd
        def _(pool):
            link = linked(pool, pool_step)
            link(nc.gpsimd.memset(ident[:, :], 0.0))
            nc.gpsimd.affine_select(out=ident[:, :], in_=ident[:, :], compare_op=ALU.not_equal, fill=1.0,
                                    base=0, pattern=[[-1, P]], channel_multiplier=1).then_inc(ident_set, 1)
            nc.gpsimd.iota(iota[:, :], [[1, P]], base=0, channel_multiplier=0,
                           allow_small_or_imprecise_dtypes=True).then_inc(iota_set, 1)
            link(nc.gpsimd.memset(mrow[:, :], 0.0))
            link(nc.gpsimd.memset(mrow[0:1, 0:CHUNK], 1.0))
            nc.gpsimd.memset(mrow[0:1, P + SEQ - CHUNK:P + SEQ], NEG).then_inc(mask_set, 1)
            pool.wait_ge(wst_in, 16)
            nc.gpsimd.affine_select(out=wst[:, :, :], in_=wst[:, :, :], compare_op=ALU.is_ge, fill=0.0,
                                    base=0, pattern=[[0, HEADS], [1, P]], channel_multiplier=-1).then_inc(wst_masked, 1)
            pool.wait_ge(k_norm, 1)
            pool.wait_ge(rows_in, 32)
            for b in range(NB):
                rk = rr[:, S_K + b * HEADS:S_K + (b + 1) * HEADS]
                link(nc.gpsimd.tensor_tensor(kv[:, b, :, 0:NOPE], kv[:, b, :, 0:NOPE], bc(rk, NOPE), ALU.mult))
                link(nc.gpsimd.tensor_tensor(kr[:, b], over_heads(lat[:, b, LAT - ROPE:LAT]), bc(rk, ROPE), ALU.mult))
                link(nc.gpsimd.tensor_tensor(kr[:, b], kr[:, b], over_heads(rows[:, R_K:R_K + ROPE]), ALU.mult))
                rotate(nc.gpsimd, link, kr[:, b], b, tmp_k, k_ready)
                if b == 0:
                    pool.wait_ge(k_ready, 1)

        @block.scalar
        def _(act):
            def split_hi(n, i, width=PIECE, per=4):
                act.wait_ge(raw_in[n % RAW], i * (per * 16 // RAW) + 16 * (n // RAW + 1))
                if n >= SPL:
                    act.wait_ge(used, i * per + (n - SPL + 1))
                nc.scalar.activation(hi[:, n % SPL, 0:width], raw[:, n % RAW, 0:width], ACT.Copy).then_inc(hi_done, 1)

            def roots(k, a, n):
                act.wait_ge(stat, k)
                nc.scalar.activation(rs[:, a:a + n], st[:, a:a + n], ACT.Sqrt).then_inc(root, 1)

            def turn_hi(s):
                to, n = splits[s][2], splits[s][4]
                for k in range(n):
                    fill = fills_before[s] + k // 2
                    act.wait_ge(turned, fill + 1)
                    nc.scalar.activation(to[:, k, :], bank[4 + fill % 4][:, (k % 2) * SEQ:(k % 2 + 1) * SEQ],
                                         ACT.Copy, scale=gain_of(s, k)).then_inc(t_hi, 1)

            def take_out(g):
                what, first, pieces, c = GROUPS[g]
                act.wait_ge(used, first + pieces)
                m = [k for k, r in enumerate(GROUPS) if r[0] == what].index(g)
                for b in range(NB):
                    f = ACT.Copy
                    if what == "cq":
                        dst = lat[:, b, 0:Q_RANK]
                    elif what == "ckv":
                        dst = lat[:, b, Q_RANK:LAT]
                    elif what in ("zv", "zu"):
                        dst, f = {"zv": zv, "zu": zu}[what][:, b, m * COLG:(m + 1) * COLG], ACT.Gelu_apprx_tanh
                    else:
                        dst = {"q": q, "kv": kv}[what][:, b].rearrange("p h n -> p (h n)")[:, m * COLG:(m + 1) * COLG]
                    ins = nc.scalar.activation(dst, bank[2 * (g % 2) + b][:, 0:c], f)
                ins.then_inc(acc_out, 1)

            def qk_evac(a, e):
                for f in range(a, e):
                    act.wait_ge(qk_turned, f + 1)
                    h = f % 6
                    to, tor = (qt, qtr) if f < 6 else (kt, ktr)
                    if h < 4:
                        dst = to[:, 2 * h:2 * h + 2, :]
                        scale = gq[:, 0:1] if f < 6 else cols[:, C_KG:C_KG + 1]
                    else:
                        dst = tor[:, 2 * (h - 4):2 * (h - 4) + 2, :]
                        scale = QSCALE if f < 6 else 1.0
                    nc.scalar.activation(dst.rearrange("p h n -> p (h n)"), bank[4 + f % 4][:, :],
                                         ACT.Copy, scale=scale).then_inc(qk_out, 1)

            def exps(b):
                nk = P * (b + 1)
                act.wait_ge(s_max, b + 1)
                if b:
                    act.wait_ge(p_turned, 2)
                for h in range(HEADS):
                    f, a = score_at(h)
                    ins = nc.scalar.activation(prob[:, h, 0:nk], bank[f][:, a:a + nk],
                                               ACT.Exp, bias=nmax[:, 1, b, h:h + 1], accum_out=sums[:, 0, b, h:h + 1])
                ins.then_inc(s_exp, 1)

            def p_evac(b):
                for f in range(2 * (b + 1)):
                    act.wait_ge(p_turned, 2 * b + f + 1)
                    if b == 0:
                        src = bank[4 + f][:, :].rearrange("p (h n) -> p h n", h=4)
                        dst = prt[:, 4 * f:4 * f + 4, 0, :]
                    else:
                        act.wait_ge(pv_ready, 2)
                        src = bank[4 + f][:, :]
                        dst = prt[:, 2 * f:2 * f + 2, :, :].rearrange("p h k n -> p (h k n)")
                    nc.scalar.activation(dst, src, ACT.Copy).then_inc(p_out, 1)

            def pv_evac(b):
                for f in range(2):
                    act.wait_ge(pv_ready, 2 * b + f + 1)
                    nc.scalar.activation(mix_hi[:, 4 * f:4 * f + 4, b * P:(b + 1) * P],
                                         bank[pv_bank(b, f)][:, :].rearrange("p (h n) -> p h n", h=4),
                                         ACT.Copy).then_inc(pv_hi, 1)

            def squares_of_x2(m):
                act.wait_ge(x2_ready, m + 1)
                for b in range(NB):
                    k = S_PART + b * 4 + m
                    ins = nc.scalar.activation(sq_x[:, b, m * COLG:(m + 1) * COLG], x[:, b, m * COLG:(m + 1) * COLG],
                                               ACT.Square, accum_out=st[:, k:k + 1])
                ins.then_inc(x2_sq, 1)

            act.wait_ge(x_in, 32)
            nc.scalar.activation(sq_x[:, 1, :], x[:, 1, :], ACT.Square,
                                 accum_out=st[:, S_X + 1:S_X + 2]).then_inc(sq_done, 1)
            roots(1, S_X, 2)
            act.wait_ge(cols_in, 16)
            turn_hi(0)
            for n in range(WQ0):
                g, what, k, pieces, c = group_of(n)
                split_hi(n, 0, KP * c)
                if k == 0 and 0 < g < 14:
                    take_out(g - 1)
                if n == 17:
                    roots(2, S_LAT, 4)
                if n == 22:
                    turn_hi(1)
                if n == 35:
                    act.wait_ge(acc_out, 10)
                    for b in range(NB):
                        nc.scalar.activation(sq_q[:, b], q[:, b], ACT.Square).then_inc(sq_done, 1)
                if n == 36:
                    for b in range(NB):
                        nc.scalar.activation(sq_k[:, b], kv[:, b, :, 0:NOPE], ACT.Square).then_inc(sq_done, 1)
                if n == 40:
                    roots(3, S_Q, 32)
                if n == 48:
                    act.wait_ge(gq_set, 1)
                    act.wait_ge(stat, 4)
                    act.wait_ge(k_ready, 2)
                    qk_evac(0, 4)
                if n == 49:
                    qk_evac(4, 8)
                    roots(4, S_V, 2)
                if n == 50:
                    qk_evac(8, 12)
                if n == 52:
                    exps(0)
                if n == 54:
                    p_evac(0)
                if n == 55:
                    pv_evac(0)
                if n == 57:
                    exps(1)
                if n == 58:
                    p_evac(1)
                    pv_evac(1)
                if n == FIRST_OUT + 4:
                    turn_hi(2)
                if k == 1 and g > 13:
                    squares_of_x2(g - 14)
            split_hi(WQ0, 0)
            squares_of_x2(3)
            roots(5, S_X2, 2)
            act.dma_start(x2_rows, x[:, :, :]).then_inc(x2_out, 16)
            turn_hi(3)

            def q_evac(i, c, first=False):
                act.wait_ge(used, i * 4 + (WQ0 + 2 * c + 2))
                if not first:
                    act.wait_ge(sc_ready, i * 2 + (c - 1))
                nc.scalar.activation(qp[:, c, :], bank[c][:, 0:SEQ], ACT.Copy).then_inc(q_out, 1)

            def wq_body(i, first):
                for p in range(4):
                    if not (first and p == 0):
                        split_hi(WQ0 + p, i)
                    if p == 0 and not first:
                        q_evac(i - 1, 1)
                    if p == 2:
                        q_evac(i, 0, first)

            def a_evac(i, c):
                act.wait_ge(used, i * 8 + (U0 + 2 * c + 2))
                nc.scalar.activation(act_all[:, bass.ds(i * 4 + c, 1), :].rearrange("p a n -> p (a n)"),
                                     bank[c % 2][:, 0:SEQ], ACT.Gelu_apprx_tanh).then_inc(a_out, 1)

            def u_body(i, first=False):
                for p in range(8):
                    split_hi(U0 + p, i, per=8)
                    if p == 0 and first:
                        q_evac(HP // 2 - 1, 1)
                        act.wait_ge(x2_out, 16)
                    elif p == 0:
                        a_evac(i - 1, 3)
                    elif p % 2 == 0:
                        a_evac(i, p // 2 - 1)

            wq_body(0, True)
            with act.Fori(1, HP // 2) as i:
                wq_body(i, False)
            u_body(0, True)
            with act.Fori(1, 23) as i:
                u_body(i)
            act.wait_ge(gate_in, 1)
            nc.scalar.activation(gate, gate, ACT.Exp).then_inc(gate_exp, 1)
            u_body(23)
            act.wait_ge(picks_turned, 1)
            nc.scalar.activation(picks[:, 0:2, :].rearrange("p a n -> p (a n)"), bank[4][:, :], ACT.Copy).then_inc(picks_out, 1)
            nc.scalar.activation(picks[:, 2, :], bank[5][:, 0:SEQ], ACT.Copy).then_inc(picks_out, 1)
            with act.Fori(24, NKEYS // 4) as i:
                u_body(i)
            a_evac(NKEYS // 4 - 1, 3)

            def c_part(i, c):
                act.wait_ge(used, i * 4 + (V0 + 2 * c - 2))
                nc.scalar.activation(c_hi[:, c, :], act_all[:, bass.ds(i * 2 + c, 1), :].rearrange("p a n -> p (a n)"),
                                     ACT.Copy).then_inc(ch_done, 1)

            act.wait_ge(g_used, 64)
            with act.Fori(0, NKEYS // 2) as i:
                for p in range(4):
                    if p % 2 == 0:
                        c_part(i, p // 2)
                    split_hi(V0 + p, i)

        @block.vector
        def _(dve):
            V = nc.vector
            link = linked(dve, dve_step)

            def split_lo(n, i, width=PIECE, per=4):
                dve.wait_ge(hi_done, i * per + (n + 1))
                V.tensor_tensor(lo[:, n % SPL, 0:width], raw[:, n % RAW, 0:width],
                                hi[:, n % SPL, 0:width].bitcast(F32), ALU.subtract).then_inc(lo_done, 1)

            def mean(a, n, width):
                return V.tensor_scalar(st[:, a:a + n], st[:, a:a + n], 1.0 / width, EPS, ALU.mult, ALU.add)

            def inverse(k, a, n):
                dve.wait_ge(root, k)
                link(V.reciprocal(rr[:, a:a + n], rs[:, a:a + n]))

            def turn_lo(s):
                to_hi, to_lo, n = splits[s][2:]
                for k in range(n):
                    fill = fills_before[s] + k // 2
                    dve.wait_ge(t_hi, 2 * (fill + 1))
                    V.scalar_tensor_tensor(to_lo[:, k, :], bank[4 + fill % 4][:, (k % 2) * SEQ:(k % 2 + 1) * SEQ],
                                           gain_of(s, k), to_hi[:, k, :].bitcast(F32),
                                           ALU.mult, ALU.subtract).then_inc(t_lo, 1)

            def scale_x(k):
                for b in range(NB):
                    ins = V.tensor_scalar(xs[:, b, :], x[:, b, :], rr[:, k + b:k + b + 1], None, ALU.mult)
                ins.then_inc(scaled, 1)

            def square_sum(junk, v, k):
                link(V.tensor_tensor_reduce(junk, v, v, 1.0, 0.0, ALU.mult, ALU.add, st[:, k:k + 1]))

            def qk_stats(s):
                if s < 2:
                    dve.wait_ge(sq_done, 2 + s)
                    k = S_Q + s * HEADS
                    link(V.tensor_reduce(st[:, k:k + HEADS], sq_q[:, s], AX.X, ALU.add))
                else:
                    b = s - 2
                    dve.wait_ge(sq_done, 4 + b)
                    k = S_K + b * HEADS
                    link(V.tensor_reduce(st[:, k:k + HEADS], sq_k[:, b], AX.X, ALU.add))
                    square_sum(sq_k[:, b, 0, 0:ROPE], lat[:, b, LAT - ROPE:LAT], S_KR + b)
                    link(V.tensor_scalar(st[:, k:k + HEADS], st[:, k:k + HEADS], st[:, S_KR + b:S_KR + b + 1], None, ALU.add))
                if s == 3:
                    mean(S_Q, 32, QK).then_inc(stat, 1)

            def score_max(b):
                nk = P * (b + 1)
                for f in range(4):
                    dve.wait_ge(s_ready, 4 * b + f + 1)
                    h = 4 * (f % 2) + f // 2
                    link(V.tensor_reduce(nmax[:, 0, b, h:h + 3:2],
                                         bank[4 + f][:, :].rearrange("p (h n) -> p h n", h=2)[:, :, 0:nk], AX.X, ALU.max))
                V.tensor_scalar(nmax[:, 1, b, :], nmax[:, 0, b, :], -1.0, None, ALU.mult).then_inc(s_max, 1)

            def softmax_scale(b):
                nk = P * (b + 1)
                dve.wait_ge(s_exp, b + 1)
                link(V.reciprocal(sums[:, 1, b, :], sums[:, 0, b, :]))
                V.tensor_tensor(prob[:, :, 0:nk], prob[:, :, 0:nk], bc(sums[:, 1, b, :], nk), ALU.mult).then_inc(p_ready, 1)

            def pv_split(b):
                for f in range(2):
                    dve.wait_ge(pv_hi, 2 * b + f + 1)
                    at_ = (slice(None), slice(4 * f, 4 * f + 4), slice(b * P, (b + 1) * P))
                    V.tensor_tensor(mix_lo[at_], bank[pv_bank(b, f)][:, :].rearrange("p (h n) -> p h n", h=4),
                                    mix_hi[at_].bitcast(F32), ALU.subtract).then_inc(pv_lo, 1)

            def gmlp_gate(b):
                for h in range(HEADS):
                    dve.wait_ge(sv_ready, 2 * b + h // 4 + 1)
                    u = zu[:, b, h * P:(h + 1) * P]
                    V.scalar_tensor_tensor(u, bank[sv_bank(b, h // 4)][:, (h % 4) * P:(h % 4 + 1) * P],
                                           cols[:, C_BS + h:C_BS + h + 1], u, ALU.add, ALU.mult).then_inc(gm_ready, 1)

            def residual(m):
                dve.wait_ge(used, FIRST_OUT + 8 * (m + 1))
                for b in range(NB):
                    xc = x[:, b, m * COLG:(m + 1) * COLG]
                    ins = V.tensor_tensor(xc, bank[2 * ((13 + m) % 2) + b][:, :], xc, ALU.add)
                ins.then_inc(x2_ready, 1)

            dve.wait_ge(x_in, 32)
            square_sum(sq_x[:, 0, :], x[:, 0, :], S_X)
            dve.wait_ge(sq_done, 1)
            mean(S_X, 2, D).then_inc(stat, 1)
            inverse(1, S_X, 2)
            scale_x(S_X)
            dve.wait_ge(cols_in, 16)
            turn_lo(0)
            V.tensor_scalar(gq[:, :], cols[:, C_QG:C_QG + 1], QSCALE, None, ALU.mult).then_inc(gq_set, 1)
            for n in range(WQ0):
                g, what, k, pieces, c = group_of(n)
                split_lo(n, 0, KP * c)
                if n == 17:
                    dve.wait_ge(acc_out, 2)
                    for b in range(NB):
                        square_sum(sq_x[:, 0, 0:Q_RANK], lat[:, b, 0:Q_RANK], S_LAT + b)
                        square_sum(sq_x[:, 0, 0:KV_RANK], lat[:, b, Q_RANK:Q_RANK + KV_RANK], S_LAT + 2 + b)
                    link(mean(S_LAT, 2, Q_RANK))
                    mean(S_LAT + 2, 2, KV_RANK).then_inc(stat, 1)
                if n == 18:
                    inverse(2, S_LAT, 4)
                    for b in range(NB):
                        for a, e, m in ((0, Q_RANK, 0), (Q_RANK, Q_RANK + KV_RANK, 2)):
                            k_ = S_LAT + m + b
                            V.tensor_scalar(lat[:, b, a:e], lat[:, b, a:e], rr[:, k_:k_ + 1], None, ALU.mult).then_inc(scaled, 1)
                if n == 22:
                    turn_lo(1)
                if 36 <= n < 40:
                    qk_stats(n - 36)
                if n == 40:
                    dve.wait_ge(root, 3)
                    V.reciprocal(rr[:, S_Q:S_Q + 32], rs[:, S_Q:S_Q + 32]).then_inc(k_norm, 1)
                    dve.wait_ge(k_norm, 1)
                if n in (41, 42):
                    b = n - 41
                    link(V.tensor_tensor(q[:, b], q[:, b], bc(rr[:, S_Q + b * HEADS:S_Q + (b + 1) * HEADS], QK), ALU.mult))
                if n in (43, 44):
                    b = n - 43
                    dve.wait_ge(rows_in, 32)
                    link(V.tensor_tensor(qr[:, b], q[:, b, :, NOPE:QK], over_heads(rows[:, R_Q:R_Q + ROPE]), ALU.mult))
                    rotate(V, link, qr[:, b], b, tmp_q, q_ready)
                    dve.wait_ge(q_ready, b + 1)
                if n in (45, 46):
                    b = n - 45
                    dve.wait_ge(acc_out, 11)
                    square_sum(tmp_q[:, 0:GW], zv[:, b, :], S_V + b)
                    if b:
                        mean(S_V, 2, GW).then_inc(stat, 1)
                if n == 50:
                    inverse(4, S_V, 2)
                if n in (50, 51):
                    b = n - 50
                    V.scalar_tensor_tensor(zv[:, b, :], zv[:, b, :], rr[:, S_V + b:S_V + b + 1], rows[:, R_V:R_V + GW],
                                           ALU.mult, ALU.mult).then_inc(v_ready, 1)
                if n == 51:
                    score_max(0)
                if n == 53:
                    softmax_scale(0)
                if n == 55:
                    pv_split(0)
                if n == 56:
                    score_max(1)
                if n == 58:
                    softmax_scale(1)
                    pv_split(1)
                if n == 59:
                    dve.wait_ge(acc_out, 13)
                    gmlp_gate(0)
                if n == 60:
                    gmlp_gate(1)
                if n == FIRST_OUT + 4:
                    turn_lo(2)
                if k == 0 and g > 13:
                    residual(g - 14)
            split_lo(WQ0, 0)
            residual(3)
            dve.wait_ge(x2_sq, 4)
            link(V.tensor_reduce(st[:, S_X2:S_X2 + 2], st[:, S_PART:S_PART + 8].rearrange("p (b m) -> p b m", b=NB), AX.X, ALU.add))
            mean(S_X2, 2, D).then_inc(stat, 1)
            inverse(5, S_X2, 2)
            scale_x(S_X2)
            turn_lo(3)

            def take_scores(i, c):
                dve.wait_ge(sc_ready, i * 2 + (c + 1))
                V.tensor_copy(score.rearrange("p (b m) -> p b m", b=NB)[:, :, bass.ds(i * 2 * NKEYS + c * NKEYS, NKEYS)],
                              bank[4 + c][:, 0:SEQ].rearrange("p (b n) -> p b n", b=NB)).then_inc(sc_out, 1)

            def wq_body(i, first):
                for p in range(4):
                    if not (first and p == 0):
                        split_lo(WQ0 + p, i)
                    if not first and p == 0:
                        take_scores(i - 1, 0)
                    if not first and p == 2:
                        take_scores(i - 1, 1)

            def u_split(i, p):
                split_lo(U0 + p, i, per=8)

            def topk_body(i):
                dve.sem_clear(dve_topk)
                link = linked(dve, dve_topk)

                def eight(out8, idx, src, values):
                    link(V.max(out8, src))
                    link(V.max_index(idx, out8, values))

                def half(a, r):
                    src = sw[:, a, :] if r == 0 else sw2
                    eight(sv[:, a * TOPK + 8 * r:a * TOPK + 8 * r + 8], i8[:, a * TOPK + 8 * r:a * TOPK + 8 * r + 8], src, src)

                def rest(a):
                    link(V.match_replace(sw2, sv[:, a * TOPK:a * TOPK + 8], sw[:, a, :], LOWEST))

                for p in range(8):
                    u_split(i, p)
                    if p == 0:
                        link(V.tensor_copy(sw.rearrange("p a n -> p (a n)"), score[:, bass.ds((i - 1) * 2 * NKEYS, 2 * NKEYS)]))
                        half(0, 0)
                    if p == 1:
                        rest(0)
                        half(0, 1)
                    if p == 2:
                        half(1, 0)
                        rest(1)
                    if p == 3:
                        half(1, 1)
                    if p == 4:
                        link(V.tensor_tensor(cand.rearrange("p (a n) -> p a n", a=TOPK), bc(sv[:, 0:TOPK], TOPK),
                                             sv[:, TOPK:2 * TOPK].unsqueeze(1).to_broadcast((P, TOPK, TOPK)), ALU.add))
                        eight(tops[:, 0:8], pos[:, 0:8], cand, cand)
                    if p == 5:
                        link(V.match_replace(cand2, tops[:, 0:8], cand, LOWEST))
                        eight(tops[:, 8:16], pos[:, 8:16], cand2, cand2)
                    if p == 6:
                        V.tensor_copy(all_top[:, bass.ds((i - 1) * TOPK, TOPK)], tops)
                        V.tensor_copy(all_pos[:, bass.ds((i - 1) * TOPK, TOPK)], pos)
                        link(V.tensor_copy(all_id[:, bass.ds((i - 1) * 2 * TOPK, 2 * TOPK)], i8))

            def pick_body(i):
                r = i - 18
                dve.sem_clear(dve_pick)
                link = linked(dve, dve_pick)
                hot4 = hot.rearrange("p (g k m) -> p g k m", g=4, k=TOPK)
                for p in range(8):
                    u_split(i, p)
                    a, s = p // 4, p % 4
                    where = posf[:, bass.ds(r * 64 + a * NTOP, 64)].rearrange("p (g k) -> p g k", g=4)
                    ids = idf[:, bass.ds(r * 128, 128)].rearrange("p (g a m) -> p g a m", g=4, a=2)[:, :, a, :]
                    full = (P, 4, TOPK, TOPK)
                    if s == 0:
                        link(V.tensor_tensor(hot4, where.unsqueeze(3).to_broadcast(full),
                                             iota[:, 0:TOPK].unsqueeze(1).unsqueeze(1).to_broadcast(full), ALU.is_equal))
                    if s == 1:
                        link(V.tensor_tensor(hot4, hot4, ids.unsqueeze(2).to_broadcast(full), ALU.mult))
                    if s == 2:
                        link(V.tensor_reduce(key_of[:, bass.ds(r * 64 + a * NTOP, 64)].rearrange("p (g k) -> p g k", g=4),
                                             hot4, AX.X, ALU.add))

            def plain_body(i):
                for p in range(8):
                    u_split(i, p)

            wq_body(0, True)
            with dve.Fori(1, HP // 2) as i:
                wq_body(i, False)
            for p in range(8):
                u_split(0, p)
                if p == 0:
                    take_scores(HP // 2 - 1, 0)
                if p == 2:
                    take_scores(HP // 2 - 1, 1)
            dve.wait_ge(sc_out, HP)
            with dve.Fori(1, 17) as i:
                topk_body(i)
            dve.wait_ge(iota_set, 1)
            late = linked(dve, dve_late)
            for p in range(8):
                u_split(17, p)
                if p == 0:
                    late(V.tensor_scalar(posu[:, 0:NTOP], all_pos, 4, None, ALU.logical_shift_right))
                    late(V.tensor_scalar(posu[:, NTOP:2 * NTOP], all_pos, TOPK - 1, None, ALU.bitwise_and))
                if p == 1:
                    late(V.tensor_copy(posf, posu))
                    late(V.tensor_copy(idf, all_id))
            with dve.Fori(18, 22) as i:
                pick_body(i)
            top3 = all_top.rearrange("p (g k) -> p g k", k=TOPK)
            gate3 = gate.rearrange("p (g k) -> p g k", k=TOPK)
            for p in range(8):
                u_split(22, p)
                if p == 0:
                    V.tensor_tensor(gate3, top3, top3[:, :, 0:1].to_broadcast((P, NB * HEADS, TOPK)), ALU.subtract).then_inc(gate_in, 1)
            for p in range(8):
                u_split(23, p)
                if p == 4:
                    dve.wait_ge(gate_exp, 1)
                    late(V.tensor_reduce(smx[:, 0:NB * HEADS], gate3, AX.X, ALU.add))
                    late(V.reciprocal(smx[:, NB * HEADS:2 * NB * HEADS], smx[:, 0:NB * HEADS]))
                    V.tensor_tensor(gate3, gate3, bc(smx[:, NB * HEADS:2 * NB * HEADS], TOPK), ALU.mult).then_inc(picks_ready, 1)
            with dve.Fori(24, NKEYS // 4) as i:
                plain_body(i)

            def hot_rows(i, s, first=False):
                if not first:
                    dve.wait_ge(g_ready, i * 2 + (s - 1))
                for t in range(4):
                    def of(a):
                        return picks[:, a, bass.ds(i * 8 + (4 * s + t), 1)]
                    V.tensor_scalar(one_i[:, s, t, :], iota[:, :], of(0), None, ALU.is_equal)
                    ins = V.tensor_scalar(one_j[:, s, t, :], iota[:, :], of(1), of(2), ALU.is_equal, ALU.mult)
                ins.then_inc(hot_ready, 1)

            def gate_rows(i, s):
                dve.wait_ge(g_ready, i * 2 + (s + 1))
                a4 = act_all[:, :, bass.ds(i * 8 + 4 * s, 4)].rearrange("p j t -> p t j")
                V.tensor_tensor(a4, bank[6 + s][:, :].rearrange("p (t j) -> p t j", t=4), a4, ALU.mult).then_inc(g_used, 1)

            dve.wait_ge(picks_out, 2)
            hot_rows(0, 0, True)
            dve.wait_ge(a_out, NKEYS)
            hot_rows(0, 1, True)
            gate_rows(0, 0)
            with dve.Fori(1, SEQ // 8) as i:
                hot_rows(i, 0)
                gate_rows(i - 1, 1)
                hot_rows(i, 1)
                gate_rows(i, 0)
            gate_rows(SEQ // 8 - 1, 1)
            dve.wait_ge(g_used, 64)

            with dve.Fori(0, NKEYS // 2) as i:
                for p in range(4):
                    if p % 2 == 0:
                        c = p // 2
                        dve.wait_ge(ch_done, i * 2 + (c + 1))
                        V.tensor_tensor(c_lo[:, c, :], act_all[:, bass.ds(i * 2 + c, 1), :].rearrange("p a n -> p (a n)"),
                                        c_hi[:, c, :].bitcast(F32), ALU.subtract).then_inc(cl_done, 1)
                    split_lo(V0 + p, i)
            dve.wait_ge(used, X0)
            for p in range(4):
                n = X0 + p
                dve.wait_ge(raw_in[n % RAW], 16 * (n // RAW + 1))
                for m in range(2):
                    r = raw[:, n % RAW, m * COLG:(m + 1) * COLG]
                    ins = V.tensor_tensor(r, bank[2 * p + m][:, :], r, ALU.add)
                ins.then_inc(y_ready, 1)

        @block.tensor
        def _(pe):
            MM = nc.tensor.matmul

            def turn(s):
                src, n = splits[s][0], splits[s][4]
                for f in range(n // 2):
                    fill = fills_before[s] + f
                    if fill >= 4:
                        pe.wait_ge(t_lo, 2 * (fill - 3))
                    for k in (2 * f, 2 * f + 1):
                        for b in range(NB):
                            m = nc.tensor.transpose(bank[4 + fill % 4][:, (k % 2) * SEQ + b * P:(k % 2) * SEQ + (b + 1) * P],
                                                    src(k, b), ident[:, :])
                    m.then_inc(turned, 1)

            def column_piece(n, i, outs, a_hi, a_lo, c, kk, first, last, skip=False):
                s = n % SPL
                pe.wait_ge(hi_done, i * 4 + (n + 1))
                parts = [(k, b, m) for k in range(kk) for b in range(NB) for m in range(len(outs[0]))]

                def w(part, k, m):
                    a = k * c + m * COLG
                    return part[:, s, a:a + min(c, COLG)]

                for k, b, m in parts:
                    MM(outs[b][m], a_hi(k, b), w(hi, k, m), start=first and k == 0, stop=False, skip_group_check=skip)
                for k, b, m in parts:
                    MM(outs[b][m], a_lo(k, b), w(hi, k, m), start=False, stop=False, skip_group_check=skip)
                pe.wait_ge(lo_done, i * 4 + (n + 1))
                for k, b, m in parts:
                    ins = MM(outs[b][m], a_hi(k, b), w(lo, k, m), start=False, stop=last and k == kk - 1, skip_group_check=skip)
                ins.then_inc(used, 1)

            def row_piece(n, i, out, half, per=4):
                s = n % SPL
                pe.wait_ge(hi_done, i * per + (n + 1))
                for k in range(8):
                    w = hi[:, s, k * P:(k + 1) * P]
                    MM(out, w, ht_hi[:, 8 * half + k, :], start=(half == 0 and k == 0), stop=False)
                    MM(out, w, ht_lo[:, 8 * half + k, :], start=False, stop=False)
                pe.wait_ge(lo_done, i * per + (n + 1))
                for k in range(8):
                    ins = MM(out, lo[:, s, k * P:(k + 1) * P], ht_hi[:, 8 * half + k, :], start=False, stop=(half == 1 and k == 7))
                ins.then_inc(used, 1)

            def turn_qk(a, e):
                for f in range(a, e):
                    if f >= 4:
                        pe.wait_ge(qk_out, f - 3)
                    if f == 0:
                        pe.wait_ge(q_ready, 2)
                    if f == 6:
                        pe.wait_ge(k_ready, 2)
                    h = f % 6
                    for r in range(2):
                        for b in range(NB):
                            if h < 4:
                                src = q[:, b, 2 * h + r, 0:NOPE] if f < 6 else kv[:, b, 2 * h + r, 0:NOPE]
                            else:
                                a2 = 2 * (2 * (h - 4) + r)
                                src = (qr if f < 6 else kr)[:, b, a2:a2 + 2, :].rearrange("p h n -> p (h n)")
                            m = nc.tensor.transpose(bank[4 + f % 4][:, r * SEQ + b * P:r * SEQ + (b + 1) * P], src, ident[:, :])
                    m.then_inc(qk_turned, 1)

            def scores(b):
                nk = P * (b + 1)
                if b == 0:
                    pe.wait_ge(qk_out, 12)
                    pe.wait_ge(mask_set, 1)
                else:
                    pe.wait_ge(p_out, 2)
                    pe.wait_ge(pv_lo, 2)
                for h in (0, 2, 4, 6, 1, 3, 5, 7):
                    f, a = score_at(h)
                    o = bank[f][:, a:a + nk]
                    r = slice(ROPE * (h % 2), ROPE * (h % 2) + ROPE)
                    MM(o, qt[:, h, b * P:(b + 1) * P], kt[:, h, 0:nk], start=True, stop=False)
                    MM(o, qtr[r, h // 2, b * P:(b + 1) * P], ktr[r, h // 2, 0:nk], start=False, stop=False)
                    m = MM(o, mrow[:, 0:P], mrow[:, P + SEQ - nk:P + SEQ], start=False, stop=True)
                    if a:
                        m.then_inc(s_ready, 1)

            def turn_p(b):
                pe.wait_ge(p_ready, b + 1)
                for h in range(HEADS):
                    for k in range(b + 1):
                        per = 4 // (b + 1)
                        f = h // per
                        a = ((h % per) * (b + 1) + k) * P
                        m = nc.tensor.transpose(bank[4 + f][:, a:a + P], prob[:, h, k * P:(k + 1) * P], ident[:, :])
                    if h % per == per - 1:
                        m.then_inc(p_turned, 1)

            def pv(b):
                pe.wait_ge(p_out, 2 if b == 0 else 6)
                for h in range(HEADS):
                    for k in range(b + 1):
                        m = MM(bank[pv_bank(b, h // 4)][:, (h % 4) * P:(h % 4 + 1) * P], kv[:, k, h, NOPE:2 * NOPE],
                               prt[:, h, k, :], start=(k == 0), stop=(k == b))
                    if h % 4 == 3:
                        m.then_inc(pv_ready, 1)

            def spatial(b):
                pe.wait_ge(v_ready, b + 1)
                if b == 0:
                    pe.wait_ge(wst_masked, 1)
                else:
                    pe.wait_ge(pv_lo, 4)
                for h in range(HEADS):
                    m = MM(bank[sv_bank(b, h // 4)][:, (h % 4) * P:(h % 4 + 1) * P], wst[:, h, :],
                           zv[:, b, h * P:(h + 1) * P], start=True, stop=True)
                    if h % 4 == 3:
                        m.then_inc(sv_ready, 1)

            pe.wait_ge(ident_set, 1)
            pe.wait_ge(scaled, 1)
            turn(0)
            for n in range(WQ0):
                g, what, k, pieces, c = group_of(n)
                if k == 0:
                    if 2 <= g < 15:
                        pe.wait_ge(acc_out, g - 1)
                    if g >= 15:
                        pe.wait_ge(x2_ready, g - 14)
                    if what in ("cq", "ckv"):
                        pe.wait_ge(t_lo, 2 * fills_before[1])
                    if what in ("q", "kv"):
                        pe.wait_ge(t_lo, 2 * fills_before[2])
                    if what == "out":
                        pe.wait_ge(pv_lo, 4)
                if what == "out" and k == 4:
                    pe.wait_ge(t_lo, 2 * fills_before[3])
                lo_k = KP * k
                if what == "q":
                    src = (ct_hi, ct_lo, lo_k)
                elif what == "kv":
                    src = (ct_hi, ct_lo, 4)
                elif what == "out":
                    src = (mix_hi, mix_lo, lo_k) if k < 4 else (ht_hi, ht_lo, lo_k - HEADS)
                else:
                    src = (ht_hi, ht_lo, lo_k)
                s_hi, s_lo, k0 = src
                column_piece(n, 0, [[bank[2 * (g % 2) + b][:, 0:c]] for b in range(NB)],
                             lambda kk, b: s_hi[:, k0 + kk, b * P:(b + 1) * P],
                             lambda kk, b: s_lo[:, k0 + kk, b * P:(b + 1) * P],
                             c, KP, k == 0, k == pieces - 1)
                if n == 20:
                    pe.wait_ge(scaled, 5)
                    turn(1)
                if n in (46, 47, 48):
                    turn_qk(4 * (n - 46), 4 * (n - 45))
                if n == 50:
                    scores(0)
                if n == 53:
                    turn_p(0)
                if n == 54:
                    pv(0)
                if n == 55:
                    scores(1)
                if n == 57:
                    turn_p(1)
                    pv(1)
                    spatial(0)
                    spatial(1)
                if n == FIRST_OUT + 3:
                    pe.wait_ge(gm_ready, 16)
                    turn(2)
            pe.wait_ge(scaled, 6)
            turn(3)
            pe.wait_ge(t_lo, 2 * fills_before[4])

            def key_scores(i, c, first=False):
                pe.wait_ge(q_out, i * 2 + (c + 1))
                if not first:
                    pe.wait_ge(sc_out, i * 2 + (c - 1))
                for b in range(NB):
                    m = MM(bank[4 + c][:, b * P:(b + 1) * P], qp[:, c, b * P:(b + 1) * P],
                           subkeys[:, bass.ds(i * 2 + c, 1), :].rearrange("p a n -> p (a n)"), start=True, stop=True)
                m.then_inc(sc_ready, 1)

            def wq_body(i, first, second=False):
                for p in range(4):
                    if p % 2 == 0 and not first:
                        pe.wait_ge(q_out, i * 2 + (p // 2 - 1))
                    row_piece(WQ0 + p, i, bank[p // 2][:, 0:SEQ], p % 2)
                    if p == 1 and not first:
                        key_scores(i - 1, 1, second)
                    if p == 3:
                        key_scores(i, 0, first)

            def u_body(i, first=False):
                for p in range(8):
                    c = p // 2
                    if p % 2 == 0 and not (first and c < 2):
                        pe.wait_ge(a_out, i * 4 + (c - 1))
                    if first and c == 0 and p == 0:
                        pe.wait_ge(q_out, HP - 1)
                    row_piece(U0 + p, i, bank[c % 2][:, 0:SEQ], p % 2, per=8)
                    if p == 1 and first:
                        key_scores(HP // 2 - 1, 1)

            pe.wait_ge(sub_in, 16)
            wq_body(0, True)
            wq_body(1, False, True)
            with pe.Fori(2, HP // 2) as i:
                wq_body(i, False)
            u_body(0, True)
            with pe.Fori(1, 24) as i:
                u_body(i)
            pe.wait_ge(picks_ready, 1)
            for a, src in enumerate((key_of[:, 0:NTOP], key_of[:, NTOP:2 * NTOP], gate)):
                for b in range(NB):
                    o = bank[4 + a // 2][:, (a % 2) * SEQ + b * P:(a % 2) * SEQ + (b + 1) * P]
                    m = nc.tensor.transpose(o, src[:, b * P:(b + 1) * P], ident[:, :])
            m.then_inc(picks_turned, 1)
            with pe.Fori(24, NKEYS // 4) as i:
                u_body(i)

            def gates(i, s, first=False):
                pe.wait_ge(hot_ready, i * 2 + (s + 1))
                if not first:
                    pe.wait_ge(g_used, i * 2 + (s - 1))
                for t in range(4):
                    m = MM(bank[6 + s][:, t * P:(t + 1) * P], one_i[:, s, t, :], one_j[:, s, t, :], start=True, stop=True)
                m.then_inc(g_ready, 1)

            gates(0, 0, True)
            gates(0, 1, True)
            with pe.Fori(1, SEQ // 8) as i:
                gates(i, 0)
                gates(i, 1)

            def v_body(i, first=False, last=False):
                for p in range(4):
                    c, h = p // 2, p % 2
                    if h == 0:
                        pe.wait_ge(cl_done, i * 2 + (c + 1))
                    column_piece(V0 + p, i, [[bank[4 * b + 2 * h + m][:, :] for m in range(2)] for b in range(NB)],
                                 lambda k, b: c_hi[:, c, b * P:(b + 1) * P], lambda k, b: c_lo[:, c, b * P:(b + 1) * P],
                                 PIECE, 1, first and c == 0, last and c == 1, skip=True)

            v_body(0, first=True)
            with pe.Fori(1, NKEYS // 2 - 1) as i:
                v_body(i)
            v_body(NKEYS // 2 - 1, last=True)


def score_at(h):
    return 4 + 2 * (h % 2) + h // 4, SEQ * (h // 2 % 2)


def pv_bank(b, f):
    return (6 if b == 0 else 4) + f


def sv_bank(b, f):
    return (6 if b == 0 else 4) + f


def column_pieces(np, w, groups, kp=KP):
    out = []
    for a, c in groups:
        m = w[:, a:a + c].reshape(-1, kp, P, c)
        out.append(np.ascontiguousarray(m.transpose(0, 2, 1, 3)).reshape(-1, P, kp * c))
    return np.concatenate(out)


def row_pieces(np, w):
    m = w.reshape(2, 8, P, -1, P)
    return np.ascontiguousarray(m.transpose(3, 0, 2, 1, 4)).reshape(-1, P, 8 * P)


def kernel(x, norm_mix_g, w_in, gmlp_vnorm_g, gmlp_ws, gmlp_bs, mla_qnorm_g, mla_w_uq,
           mla_kvnorm_g, mla_w_ukv, mla_qk_q_g, mla_qk_k_g, w_out, norm_ffn_g,
           peer_w_q, peer_subkeys, peer_u, peer_v):
    import numpy as np
    import concourse.bacc as bacc
    from concourse.bass_utils import run_bass_kernel_spmd

    def col(g):
        return g.reshape(-1, P).T

    w = w_in[0]
    two = [(k * COLG, COLG) for k in range(2)]
    wo = np.concatenate([w_out[0, GW:], w_out[0, :GW]])
    pos = np.arange(SEQ, dtype=np.float32)
    inv = (np.float32(10000.0) ** (-np.arange(0, ROPE, 2, dtype=np.float32) / np.float32(ROPE))).astype(np.float32)
    ang = pos[:, None] * inv[None, :]
    rope = np.stack([np.cos(ang), np.sin(ang)], 1).astype(np.float32)
    arrays = {
        "x": x.reshape(SEQ, D),
        "w_cq": column_pieces(np, w, [(2 * GW, Q_RANK)]),
        "w_ckv": column_pieces(np, w, [(2 * GW + Q_RANK, KV_RANK + ROPE)]),
        "w_zv": column_pieces(np, w, [(GW + a, c) for a, c in two]),
        "w_zu": column_pieces(np, w, two),
        "w_out": column_pieces(np, wo, [(k * COLG, COLG) for k in range(4)]),
        "w_kv": column_pieces(np, mla_w_ukv[0], [(k * COLG, COLG) for k in range(4)]),
        "w_uq": column_pieces(np, mla_w_uq[0], [(k * COLG, COLG) for k in range(3)]),
        "w_pq": row_pieces(np, peer_w_q[0]),
        "peer_u": np.ascontiguousarray(
            peer_u[0].reshape(P, NKEYS, 2, 8, P).transpose(1, 2, 4, 3, 0)).reshape(-1, P, PIECE),
        "peer_v": np.ascontiguousarray(
            peer_v[0].reshape(P, NKEYS, 2, PIECE).transpose(1, 2, 0, 3)).reshape(-1, P, PIECE),
        "subkeys": np.ascontiguousarray(peer_subkeys[0].reshape(HP, NKEYS, P).transpose(2, 0, 1)),
        "ws": np.ascontiguousarray(gmlp_ws[0].transpose(2, 0, 1)),
        "rope": np.ascontiguousarray(rope.reshape(NB, P, 2, ROPE // 2).transpose(1, 0, 2, 3)),
        "cols": np.ascontiguousarray(np.concatenate(
            [col(norm_mix_g[0]), col(norm_ffn_g[0]), col(mla_qnorm_g[0]), col(mla_kvnorm_g[0]),
             col(mla_qk_q_g[0, :NOPE]), col(mla_qk_k_g[0, :NOPE]), gmlp_bs[0].T], axis=1)),
        "rows": np.concatenate([gmlp_vnorm_g[0], mla_qk_q_g[0, NOPE:], mla_qk_k_g[0, NOPE:]]).reshape(1, NROWS),
    }
    nc = bacc.Bacc("TRN2", target_bir_lowering=False, num_devices=1, dynamic_dma_scratch_size=4096)
    d = {}
    for name, a in arrays.items():
        d[name] = nc.dram_tensor(f"in_{name}", a.shape, mybir.dt.from_np(a.dtype), kind="ExternalInput").ap()
    d["x2"] = nc.dram_tensor("x2_scratch", (SEQ, D), F32, kind="Internal").ap()
    out = nc.dram_tensor("out_y", (SEQ, D), F32, kind="ExternalOutput").ap()
    build(nc, d, out)
    r = run_bass_kernel_spmd(nc, [{f"in_{name}": a for name, a in arrays.items()}], core_ids=[0])
    return r.results[0]["out_y"].reshape(1, SEQ, D)
```

```python
from contextlib import ExitStack

import concourse.bass as bass
from concourse import mybir

F32 = mybir.dt.float32
F32R = mybir.dt.float32r
U32 = mybir.dt.uint32
ALU = mybir.AluOpType
ACT = mybir.ActivationFunctionType
AX = mybir.AxisListType

P = 128
SEQ = 256
D = 2048
NB = SEQ // P
KD = D // P
HEADS = 8
NOPE, ROPE, QK = 128, 64, 192
Q_RANK, KV_RANK = 512, 256
LAT = Q_RANK + KV_RANK + ROPE
GW = 1024
CHUNK = 64
NKEYS = 128
TOPK = 16
HP = 16
EPS = 1e-6
QSCALE = float(QK) ** -0.5
NEG = -1.0e30
LOWEST = -3.0e38

PIECE = 1024
RAW = 4
SPL = 2
COLG = 512
QK_ORDER = (0, 1, 2, 3, 6, 7, 8, 9, 4, 5, 10, 11)
X_CUTS = (0, 256, 512, 1024, 1536, 2048)

KP = 2
GROUPS = []


def _groups():
    n = 0
    for what, pieces, cols in (
        [("cq", 8, Q_RANK), ("ckv", 8, KV_RANK + ROPE), ("zv", 8, COLG)] + [("q", 2, COLG)] * 3
        + [("kv", 1, COLG)] * 4 + [("zv", 8, COLG)] + [("zu", 8, COLG)] * 2 + [("out", 8, COLG)] * 4
    ):
        GROUPS.append((what, n, pieces, cols))
        n += pieces
    return n


WQ0 = _groups()
U0 = WQ0 + 2 * HP
V0 = U0 + 2 * NKEYS
X0 = V0 + 2 * NKEYS
FIRST_OUT = GROUPS[13][1]

C_MIX, C_FFN, C_QN, C_KVN, C_QG, C_KG, C_BS = 0, 16, 32, 36, 38, 39, 40
NCOLS = 48
R_V, R_Q, R_K = 0, GW, GW + ROPE
NROWS = GW + 2 * ROPE


def build(nc, d, out):
    ctx = ExitStack()
    front_ctx = ExitStack()
    wq_ctx = ExitStack()

    def sb(name, shape, dt=F32, c=ctx):
        return c.enter_context(nc.sbuf_tensor(name, shape, dt))

    def sem(name):
        return ctx.enter_context(nc.semaphore(name))

    with ctx:
        raw = sb("raw", [P, RAW, PIECE])
        hi = sb("hi", [P, SPL, PIECE], F32R)
        lo = sb("lo", [P, SPL, PIECE], F32R)
        ht = sb("ht", [P, KD, 2, SEQ], F32R)
        ht_hi, ht_lo = ht[:, :, 0, :], ht[:, :, 1, :]
        ident = sb("ident", [P, P])
        iota = sb("iota", [P, P])
        cols = sb("cols", [P, NCOLS])
        rows = sb("rows", [P, NROWS])
        rope = sb("rope", [P, NB, 2, ROPE // 2])
        wst = sb("wst", [P, HEADS, P])
        st = sb("st", [P, 64])
        rs = sb("rs", [P, 64])
        rr = sb("rr", [P, 64])
        nmax = sb("nmax", [P, 2, NB, HEADS])
        sums = sb("sums", [P, 2, NB, HEADS])
        gq = sb("gq", [P, 1])
        mrow = sb("mrow", [P, P + SEQ])
        picks = sb("picks", [P, 3, SEQ])
        hot_own = sb("hot_own", [P, 2, 2, 4, P])
        keys_pool = sb("keys_pool", [P, 4, 2])
        c_hi = sb("c_hi", [P, 2, SEQ], F32R)
        c_lo = sb("c_lo", [P, 2, SEQ], F32R)
        bank = [ctx.enter_context(nc.psum_tensor(f"bank{i}", [P, COLG], F32)) for i in range(8)]

        hots = [hot_own[:, s] for s in range(2)] + [
            v.rearrange("p (a t n) -> p a t n", a=2, t=4)
            for v in (wst[:, :, :].rearrange("p h n -> p (h n)"), rows[:, 0:HEADS * P])]
        one_i = [h[:, 0] for h in hots]
        one_j = [h[:, 1] for h in hots]

        a_part = rows[:, 0:2 * SEQ].rearrange("p (c n) -> p c n", c=2)

        FRONT = 24192 + NB * HEADS * ROPE
        front = sb("front", [P, FRONT], F32, front_ctx)
        mix_hi = sb("mix_hi", [P, HEADS, SEQ], F32R, front_ctx)
        mix_lo = sb("mix_lo", [P, HEADS, SEQ], F32R, front_ctx)
        ct_hi = sb("ct_hi", [P, 6, SEQ], F32R, front_ctx)
        ct_lo = sb("ct_lo", [P, 6, SEQ], F32R, front_ctx)
        front_ctx.close()
        htw_hi = sb("htw_hi", [P, KD, SEQ], F32R, wq_ctx)
        htw_lo = sb("htw_lo", [P, KD, SEQ], F32R, wq_ctx)
        full = sb("full", [P, KD // 4, SEQ], F32, wq_ctx)
        norm_rows = sb("norm_rows", [P, 3, P], F32, wq_ctx)
        wq_ctx.close()
        act_all = sb("act_all", [P, NKEYS, SEQ])

        at = [0]

        def cut(*shape):
            n = 1
            for s in shape:
                n *= s
            v = front[:, at[0]:at[0] + n]
            at[0] += n
            names = "abcd"[:len(shape)]
            return v.rearrange(f"p ({' '.join(names)}) -> p {' '.join(names)}",
                               **dict(zip(names[1:], shape[1:])))

        qt = cut(HEADS, SEQ)
        qtr = cut(HEADS // 2, SEQ)
        kt = cut(HEADS, SEQ)
        ktr = cut(HEADS // 2, SEQ)
        squares = front[:, 0:at[0]]
        kv = cut(NB, HEADS, 2 * NOPE)
        z0 = at[0]
        zv = cut(NB, GW)
        zu = cut(NB, GW)
        sq_x2 = front[:, z0:z0 + NB * D].rearrange("p (b n) -> p b n", b=NB)
        q0 = at[0]
        q = cut(NB, HEADS, QK)
        kr = cut(NB, HEADS, ROPE)
        lat = cut(NB, LAT)
        prob = front[:, q0:q0 + HEADS * SEQ].rearrange("p (h n) -> p h n", h=HEADS)
        prt = front[:, q0 + HEADS * SEQ:q0 + 2 * HEADS * SEQ].rearrange("p (h k n) -> p h k n", h=HEADS, k=2)
        x = cut(NB, D)
        qr = cut(NB, HEADS, ROPE)
        assert at[0] == FRONT
        sq_x = squares[:, 0:NB * D].rearrange("p (b n) -> p b n", b=NB)
        sq_q = squares[:, 0:NB * HEADS * QK].rearrange("p (b h n) -> p b h n", b=NB, h=HEADS)
        sq_k = squares[:, NB * HEADS * QK:NB * HEADS * (QK + NOPE)].rearrange("p (b h n) -> p b h n", b=NB, h=HEADS)
        tmp_q, tmp_k = zu[:, 0, :], zu[:, 1, :]

        LAST_FREE = 96
        flat = act_all[:, LAST_FREE:NKEYS, :].rearrange("p j t -> p (j t)")
        NTOP = NB * HEADS * TOPK
        sat = [0]

        def scratch(n):
            v = flat[:, sat[0]:sat[0] + n]
            sat[0] += n
            return v

        keys_at = scratch(HP * NKEYS)
        subkeys = keys_at.rearrange("p (h n) -> p h n", h=HP)
        score = scratch(NB * HP * NKEYS)
        qp_at = scratch(2 * SEQ)
        qp = qp_at.rearrange("p (c n) -> p c n", c=2)
        sw = scratch(2 * NKEYS).rearrange("p (a n) -> p a n", a=2)
        sw2 = scratch(NKEYS)
        cand = scratch(TOPK * TOPK)
        cand2 = scratch(TOPK * TOPK)
        sv = scratch(2 * TOPK)
        tops = scratch(TOPK)
        i8 = scratch(2 * TOPK).bitcast(U32)
        pos = scratch(TOPK).bitcast(U32)
        assert sat[0] <= (NKEYS - LAST_FREE) * SEQ
        all_top = keys_at[:, 0:NTOP]
        all_pos = keys_at[:, NTOP:2 * NTOP].bitcast(U32)
        all_id = keys_at[:, 2 * NTOP:4 * NTOP].bitcast(U32)
        idf = keys_at[:, 4 * NTOP:6 * NTOP]
        posu = keys_at[:, 6 * NTOP:8 * NTOP].bitcast(U32)
        posf = qp_at[:, 0:2 * NTOP]
        hot = score[:, 0:1024]
        key_of = score[:, 1024:1024 + 2 * NTOP]
        gate = score[:, 1536:1536 + NTOP]
        smx = score[:, 1792:1792 + 2 * NB * HEADS]

        S_X, S_LAT, S_Q, S_K, S_V, S_X2, S_PART, S_KR = 0, 2, 6, 22, 38, 40, 42, 50

        cols_in = sem("cols_in")
        rows_in = sem("rows_in")
        wst_in = sem("wst_in")
        x_in = [sem(f"x_in{i}") for i in range(len(X_CUTS) - 1)]
        sub_in = sem("sub_in")
        x2_out = sem("x2_out")
        raw_in = [sem(f"raw_in{i}") for i in range(RAW)]
        hi_done = sem("hi_done")
        lo_done = sem("lo_done")
        used = sem("used")
        ident_set = sem("ident_set")
        iota_set = sem("iota_set")
        mask_set = sem("mask_set")
        wst_masked = sem("wst_masked")
        turned = sem("turned")
        t_hi = sem("t_hi")
        t_lo = sem("t_lo")
        acc_out = sem("acc_out")
        stat = sem("stat")
        root = sem("root")
        x_rms = sem("x_rms")
        scaled = sem("scaled")
        sq_done = sem("sq_done")
        q_norm = sem("q_norm")
        q_ready = sem("q_ready")
        k_norm = sem("k_norm")
        k_ready = sem("k_ready")
        gq_set = sem("gq_set")
        qk_turned = sem("qk_turned")
        qk_out = sem("qk_out")
        s_ready = sem("s_ready")
        s_max = sem("s_max")
        s_exp = sem("s_exp")
        p_ready = sem("p_ready")
        p_turned = sem("p_turned")
        p_out = sem("p_out")
        pv_ready = sem("pv_ready")
        pv_hi = sem("pv_hi")
        pv_lo = sem("pv_lo")
        v_ready = sem("v_ready")
        sv_ready = sem("sv_ready")
        gm_ready = sem("gm_ready")
        x2_ready = sem("x2_ready")
        x2_sq = sem("x2_sq")
        diag_set = sem("diag_set")
        rms_row = sem("rms_row")
        full_sum = sem("full_sum")
        full_norm = sem("full_norm")
        n_hi = sem("n_hi")
        n_lo = sem("n_lo")
        q_out = sem("q_out")
        sc_ready = sem("sc_ready")
        sc_out = sem("sc_out")
        a_rest = sem("a_rest")
        a_sum = sem("a_sum")
        a_out = sem("a_out")
        gate_in = sem("gate_in")
        gate_exp = sem("gate_exp")
        picks_ready = sem("picks_ready")
        picks_turned = sem("picks_turned")
        picks_out = sem("picks_out")
        hot_j = sem("hot_j")
        hot_gated = sem("hot_gated")
        hot_i = sem("hot_i")
        hot_i2 = sem("hot_i2")
        keys_at_pool = sem("keys_at_pool")
        g_ready = sem("g_ready")
        g_used = sem("g_used")
        ch_done = sem("ch_done")
        cl_done = sem("cl_done")
        y_ready = sem("y_ready")
        y_sent = sem("y_sent")
        dve_step = sem("dve_step")
        dve_topk = sem("dve_topk")
        dve_pick = sem("dve_pick")
        dve_late = sem("dve_late")
        pool_step = sem("pool_step")
        pool_sets = sem("pool_sets")

        x_rows = d["x"].rearrange("(b p) n -> p b n", p=P)
        x2_rows = d["x2"].rearrange("(b p) n -> p b n", p=P)
        out_rows = out.rearrange("(b p) n -> p b n", p=P)

        def group_of(n):
            for g, (what, first, pieces, c) in enumerate(GROUPS):
                if first <= n < first + pieces:
                    return g, what, n - first, pieces, c

        def linked(eng, s, base=0):
            count = [0]

            def link(ins):
                count[0] += 1
                ins.then_inc(s, 1)
                eng.wait_ge(s, base + count[0])
            return link

        def bc(v, n):
            return v.unsqueeze(2).to_broadcast((v.shape[0], v.shape[1], n))

        def over_heads(v):
            return v.unsqueeze(1).to_broadcast((P, HEADS, v.shape[1]))

        def rotate(e, link, v, b, tmp, done, products=True, sums=True):
            h = ROPE // 2
            cos, sin = over_heads(rope[:, b, 0, :]), over_heads(rope[:, b, 1, :])
            t = [tmp[:, k * HEADS * h:(k + 1) * HEADS * h].rearrange("p (h n) -> p h n", h=HEADS) for k in range(4)]
            if products:
                link(e.tensor_tensor(t[0], v[:, :, 0:h], cos, ALU.mult))
                link(e.tensor_tensor(t[1], v[:, :, h:2 * h], sin, ALU.mult))
                link(e.tensor_tensor(t[2], v[:, :, 0:h], sin, ALU.mult))
                link(e.tensor_tensor(t[3], v[:, :, h:2 * h], cos, ALU.mult))
            if sums:
                link(e.tensor_tensor(v[:, :, 0:h], t[0], t[1], ALU.subtract))
                e.tensor_tensor(v[:, :, h:2 * h], t[2], t[3], ALU.add).then_inc(done, 1)

        splits = [
            (lambda k, b: x[:, b, k * P:(k + 1) * P], C_MIX, ht_hi, ht_lo, KD),
            (lambda k, b: lat[:, b, k * P:(k + 1) * P], C_QN, ct_hi, ct_lo, 6),
            (lambda k, b: zu[:, b, k * P:(k + 1) * P], None, ht_hi, ht_lo, HEADS),
            (lambda k, b: x[:, b, k * P:(k + 1) * P], C_FFN, htw_hi, htw_lo, KD),
        ]
        fills_before = [0]
        for s in splits:
            fills_before.append(fills_before[-1] + s[4] // 2)

        def fill_bank(s, fill):
            return bank[fill % 2] if s == 2 else bank[4 + fill % 4]

        def gain_of(s, k):
            gain = splits[s][1]
            return 1.0 if gain is None else cols[:, gain + k:gain + k + 1]

        block = ctx.enter_context(nc.Block())

        @block.sync
        def _(sp):
            def load_x(c):
                a, e = X_CUTS[c:c + 2]
                sp.dma_start(x[:, :, a:e], x_rows[:, :, a:e]).then_inc(x_in[c], 16)

            def load(n, i, src, width=PIECE):
                if n >= RAW:
                    sp.wait_ge(lo_done, i * 4 + (n - RAW + 1))
                sp.dma_start(raw[:, n % RAW, 0:width], src).then_inc(raw_in[n % RAW], 16)

            seen = {}
            load_x(0)
            sp.dma_start(cols[:, :], d["cols"]).then_inc(cols_in, 16)
            for n in range(WQ0):
                if 0 < n < len(X_CUTS) - 1:
                    load_x(n)
                g, what, k, pieces, c = group_of(n)
                m = seen.get(what, 0)
                seen[what] = m + 1
                load(n, 0, d["w_uq" if what == "q" else "w_" + what][m], KP * c)
                if n == 8:
                    sp.dma_start(rows[:, :], d["rows"].to_broadcast((P, NROWS))).then_inc(rows_in, 16)
                    sp.dma_start(rope[:, :, :, :], d["rope"]).then_inc(rows_in, 16)
                    sp.dma_start(wst[:, :, :], d["ws"]).then_inc(wst_in, 16)
            for p in range(4):
                load(WQ0 + p, 0, d["w_pq"][p])
            sp.wait_ge(used, WQ0)
            sp.dma_start(subkeys, d["subkeys"]).then_inc(sub_in, 16)

            def four(first, i, src):
                for p in range(4):
                    load(first + p, i, src[bass.ds(i * 4 + p, 1)].rearrange("a p n -> (a p) n"))

            with sp.Fori(1, HP // 2) as i:
                four(WQ0, i, d["w_pq"])
            with sp.Fori(0, NKEYS // 2) as i:
                four(U0, i, d["peer_u"])
            with sp.Fori(0, NKEYS // 2) as i:
                four(V0, i, d["peer_v"])
            sp.wait_ge(x2_out, 16)
            for p in range(4):
                load(X0 + p, 0, x2_rows[:, p % 2, (p // 2) * PIECE:(p // 2 + 1) * PIECE])
            for p in range(4):
                for m in range(2):
                    a = (p // 2) * PIECE + m * COLG
                    sp.wait_ge(y_ready, 2 * p + m + 1)
                    sp.dma_start(out_rows[:, p % 2, a:a + COLG],
                                 raw[:, (X0 + p) % RAW, m * COLG:(m + 1) * COLG]).then_inc(y_sent, 16)
            sp.wait_ge(y_sent, 8 * 16)

        @block.gpsimd
        def _(pool):
            link = linked(pool, pool_step)
            link(nc.gpsimd.memset(ident[:, :], 0.0))
            nc.gpsimd.affine_select(out=ident[:, :], in_=ident[:, :], compare_op=ALU.not_equal, fill=1.0,
                                    base=0, pattern=[[-1, P]], channel_multiplier=1).then_inc(ident_set, 1)
            nc.gpsimd.iota(iota[:, :], [[1, P]], base=0, channel_multiplier=0,
                           allow_small_or_imprecise_dtypes=True).then_inc(iota_set, 1)
            link(nc.gpsimd.memset(mrow[:, :], 0.0))
            link(nc.gpsimd.memset(mrow[0:1, 0:CHUNK], 1.0))
            nc.gpsimd.memset(mrow[0:1, P + SEQ - CHUNK:P + SEQ], NEG).then_inc(mask_set, 1)
            pool.wait_ge(wst_in, 16)
            nc.gpsimd.affine_select(out=wst[:, :, :], in_=wst[:, :, :], compare_op=ALU.is_ge, fill=0.0,
                                    base=0, pattern=[[0, HEADS], [1, P]], channel_multiplier=-1).then_inc(wst_masked, 1)
            pool.wait_ge(k_norm, 1)
            pool.wait_ge(rows_in, 32)
            for b in range(NB):
                rk = rr[:, S_K + b * HEADS:S_K + (b + 1) * HEADS]
                link(nc.gpsimd.tensor_tensor(kv[:, b, :, 0:NOPE], kv[:, b, :, 0:NOPE], bc(rk, NOPE), ALU.mult))
                link(nc.gpsimd.tensor_tensor(kr[:, b], over_heads(lat[:, b, LAT - ROPE:LAT]), bc(rk, ROPE), ALU.mult))
                link(nc.gpsimd.tensor_tensor(kr[:, b], kr[:, b], over_heads(rows[:, R_K:R_K + ROPE]), ALU.mult))
                rotate(nc.gpsimd, link, kr[:, b], b, tmp_k, k_ready)
                if b == 0:
                    pool.wait_ge(k_ready, 1)

            def hot_rows(i, s, first=False):
                pool.wait_ge(keys_at_pool, i * 4 + (s + 1))
                if not first:
                    pool.wait_ge(g_ready, i * 4 + (s - 3))
                pool.sem_inc(pool_sets, 1)
                for t in (2, 3):
                    ins = nc.gpsimd.tensor_scalar(one_i[s][:, t, :], iota[:, :],
                                                  keys_pool[:, s, t - 2:t - 1], None, ALU.is_equal)
                ins.then_inc(hot_i2, 1)

            for s in range(3):
                hot_rows(0, s, True)
            pool.wait_ge(a_out, NKEYS)
            hot_rows(0, 3, True)
            with pool.Fori(1, SEQ // 16) as i:
                for s in range(4):
                    hot_rows(i, s)

        @block.scalar
        def _(act):
            def split_hi(n, i, width=PIECE, per=4):
                act.wait_ge(raw_in[n % RAW], i * (per * 16 // RAW) + 16 * (n // RAW + 1))
                if n >= SPL:
                    act.wait_ge(used, i * per + (n - SPL + 1))
                nc.scalar.activation(hi[:, n % SPL, 0:width], raw[:, n % RAW, 0:width], ACT.Copy).then_inc(hi_done, 1)

            def roots(k, a, n):
                act.wait_ge(stat, k)
                nc.scalar.activation(rs[:, a:a + n], st[:, a:a + n], ACT.Sqrt).then_inc(root, 1)

            def turn_hi(s, a, e):
                to = splits[s][2]
                for k in range(2 * a, 2 * e):
                    fill = fills_before[s] + k // 2
                    act.wait_ge(turned, fill + 1)
                    nc.scalar.activation(to[:, k, :], fill_bank(s, fill)[:, (k % 2) * SEQ:(k % 2 + 1) * SEQ],
                                         ACT.Copy, scale=gain_of(s, k)).then_inc(t_hi, 1)

            def take_out(g):
                what, first, pieces, c = GROUPS[g]
                act.wait_ge(used, first + pieces)
                m = [k for k, r in enumerate(GROUPS) if r[0] == what].index(g)
                if g == 0:
                    act.wait_ge(x_rms, 1)
                for b in range(NB):
                    f, r = ACT.Copy, 1.0 if what in ("q", "kv") else rr[:, S_X + b:S_X + b + 1]
                    if what == "cq":
                        dst = lat[:, b, 0:Q_RANK]
                    elif what == "ckv":
                        dst = lat[:, b, Q_RANK:LAT]
                    elif what in ("zv", "zu"):
                        dst, f = {"zv": zv, "zu": zu}[what][:, b, m * COLG:(m + 1) * COLG], ACT.Gelu_apprx_tanh
                    else:
                        dst = {"q": q, "kv": kv}[what][:, b].rearrange("p h n -> p (h n)")[:, m * COLG:(m + 1) * COLG]
                    ins = nc.scalar.activation(dst, bank[2 * (g % 2) + b][:, 0:c], f, scale=r)
                ins.then_inc(acc_out, 1)

            def qk_evac(a, e):
                for j in range(a, e):
                    act.wait_ge(qk_turned, j + 1)
                    f = QK_ORDER[j]
                    h = f % 6
                    to, tor = (qt, qtr) if f < 6 else (kt, ktr)
                    if h < 4:
                        dst = to[:, 2 * h:2 * h + 2, :]
                        scale = gq[:, 0:1] if f < 6 else cols[:, C_KG:C_KG + 1]
                    else:
                        dst = tor[:, 2 * (h - 4):2 * (h - 4) + 2, :]
                        scale = QSCALE if f < 6 else 1.0
                    nc.scalar.activation(dst.rearrange("p h n -> p (h n)"), bank[4 + j % 4][:, :],
                                         ACT.Copy, scale=scale).then_inc(qk_out, 1)

            def exps(b):
                nk = P * (b + 1)
                act.wait_ge(s_max, b + 1)
                if b:
                    act.wait_ge(p_turned, 2)
                for h in range(HEADS):
                    f, a = score_at(h)
                    ins = nc.scalar.activation(prob[:, h, 0:nk], bank[f][:, a:a + nk],
                                               ACT.Exp, bias=nmax[:, 1, b, h:h + 1], accum_out=sums[:, 0, b, h:h + 1])
                ins.then_inc(s_exp, 1)

            def p_evac(b):
                for f in range(2 * (b + 1)):
                    act.wait_ge(p_turned, 2 * b + f + 1)
                    if b == 0:
                        src = bank[4 + f][:, :].rearrange("p (h n) -> p h n", h=4)
                        dst = prt[:, 4 * f:4 * f + 4, 0, :]
                    else:
                        act.wait_ge(pv_ready, 2)
                        src = bank[4 + f][:, :]
                        dst = prt[:, 2 * f:2 * f + 2, :, :].rearrange("p h k n -> p (h k n)")
                    nc.scalar.activation(dst, src, ACT.Copy).then_inc(p_out, 1)

            def pv_evac(b):
                for f in range(2):
                    act.wait_ge(pv_ready, 2 * b + f + 1)
                    nc.scalar.activation(mix_hi[:, 4 * f:4 * f + 4, b * P:(b + 1) * P],
                                         bank[pv_bank(b, f)][:, :].rearrange("p (h n) -> p h n", h=4),
                                         ACT.Copy).then_inc(pv_hi, 1)

            def squares_of_x2(m):
                act.wait_ge(x2_ready, m + 1)
                for b in range(NB):
                    k = S_PART + b * 4 + m
                    ins = nc.scalar.activation(sq_x2[:, b, m * COLG:(m + 1) * COLG], x[:, b, m * COLG:(m + 1) * COLG],
                                               ACT.Square, accum_out=st[:, k:k + 1])
                ins.then_inc(x2_sq, 1)

            act.wait_ge(cols_in, 16)
            for n in range(WQ0):
                g, what, k, pieces, c = group_of(n)
                if n < KD // 2:
                    turn_hi(0, n, n + 1)
                split_hi(n, 0, KP * c)
                if n == 4:
                    for x_part in x_in:
                        act.wait_ge(x_part, 16)
                    nc.scalar.activation(sq_x[:, 1, :], x[:, 1, :], ACT.Square,
                                         accum_out=st[:, S_X + 1:S_X + 2]).then_inc(sq_done, 1)
                if n == 6:
                    roots(1, S_X, 2)
                if k == 0 and 0 < g < 14:
                    take_out(g - 1)
                if n == 17:
                    roots(2, S_LAT, 4)
                if n == 22:
                    turn_hi(1, 0, 3)
                if n in (31, 33):
                    b = (n - 31) // 2
                    act.wait_ge(acc_out, 6)
                    nc.scalar.activation(sq_q[:, b], q[:, b], ACT.Square).then_inc(sq_done, 1)
                if n == 35:
                    act.wait_ge(acc_out, 10)
                    for b in range(NB):
                        nc.scalar.activation(sq_k[:, b], kv[:, b, :, 0:NOPE], ACT.Square).then_inc(sq_done, 1)
                if n == 38:
                    roots(3, S_Q, 32)
                if n == 43:
                    act.wait_ge(gq_set, 1)
                if n in (43, 44, 45):
                    qk_evac(4 * (n - 43), 4 * (n - 42))
                if n == 47:
                    roots(4, S_V, 2)
                if n == 48:
                    exps(0)
                if n == 50:
                    p_evac(0)
                if n == 51:
                    pv_evac(0)
                if n == 53:
                    exps(1)
                if n == 55:
                    p_evac(1)
                if n == 57:
                    pv_evac(1)
                if FIRST_OUT + 3 <= n < FIRST_OUT + 7:
                    turn_hi(2, n - FIRST_OUT - 3, n - FIRST_OUT - 2)
                if k == 1 and g > 13:
                    squares_of_x2(g - 14)
                if k == 3 and g > 13:
                    turn_hi(3, 2 * (g - 14), 2 * (g - 13))

            def q_evac(i, c, first=False):
                act.wait_ge(used, i * 4 + (WQ0 + c + 3))
                if not first:
                    act.wait_ge(sc_ready, i * 2 + (c - 1))
                nc.scalar.activation(qp[:, c, :], bank[2 + c][:, 0:SEQ], ACT.Copy).then_inc(q_out, 1)

            def wq_body(i, first=False, norm=False):
                for p in range(4):
                    split_hi(WQ0 + p, i)
                    if p == 0:
                        q_evac(i - 1, 1, first)
                    if p == 2 and norm:
                        act.wait_ge(full_norm, i * 1)
                        nc.scalar.activation(ht_hi[:, bass.ds(i * 4 - 4, 4), :], full[:, :, :], ACT.Copy).then_inc(n_hi, 1)
                    if p == 3:
                        q_evac(i, 0)

            def a_half(i, c):
                act.wait_ge(used, i * 8 + (U0 + 2 * c + 2))
                nc.scalar.activation(a_part[:, c % 2, :], bank[c % 2][:, SEQ:2 * SEQ], ACT.Copy).then_inc(a_rest, 1)

            def a_gelu(i, c):
                act.wait_ge(a_sum, i * 4 + (c + 1))
                nc.scalar.activation(act_all[:, bass.ds(i * 4 + c, 1), :].rearrange("p a n -> p (a n)"),
                                     a_part[:, c % 2, :], ACT.Gelu_apprx_tanh).then_inc(a_out, 1)

            def u_body(i, first=False, take_picks=False):
                for p in range(8):
                    split_hi(U0 + p, i, per=8)
                    if p == 0 and take_picks:
                        act.wait_ge(picks_turned, 1)
                        nc.scalar.activation(picks[:, 0:2, :].rearrange("p a n -> p (a n)"), bank[4][:, :], ACT.Copy).then_inc(picks_out, 1)
                        nc.scalar.activation(picks[:, 2, :], bank[5][:, 0:SEQ], ACT.Copy).then_inc(picks_out, 1)
                    if p == 0 and first:
                        q_evac(HP // 2 - 1, 1)
                        act.wait_ge(x2_out, 16)
                    elif p > 1 or not first:
                        (a_half if p % 2 == 0 else a_gelu)(i - (p < 2), (p // 2 - 1) % 4)

            for p in range(4):
                split_hi(WQ0 + p, 0)
                if p == 1:
                    turn_hi(3, 6, 8)
                if p == 2:
                    squares_of_x2(3)
                    act.dma_start(x2_rows, x[:, :, :]).then_inc(x2_out, 16)
                if p == 3:
                    roots(5, S_X2, 2)
                    q_evac(0, 0, True)
            wq_body(1, True, True)
            with act.Fori(2, 5) as i:
                wq_body(i, norm=True)
            with act.Fori(5, HP // 2) as i:
                wq_body(i)
            u_body(0, True)
            with act.Fori(1, 23) as i:
                u_body(i)
            act.wait_ge(gate_in, 1)
            nc.scalar.activation(gate, gate, ACT.Exp).then_inc(gate_exp, 1)
            u_body(23)
            u_body(24, take_picks=True)
            with act.Fori(25, NKEYS // 4) as i:
                u_body(i)

            def send_keys(i, s):
                if i is not None:
                    act.wait_ge(hot_i2, i * 4 + (s + 1))
                    t0 = i * 16 + (16 + 4 * s + 2)
                else:
                    t0 = 4 * s + 2
                nc.scalar.activation(keys_pool[:, s, :], picks[:, 0, bass.ds(t0, 2)], ACT.Copy).then_inc(keys_at_pool, 1)

            def hot_gates(i, s):
                act.wait_ge(hot_j, i * 4 + (s + 1))
                for t in range(4):
                    ins = nc.scalar.activation(one_j[s][:, t, :], one_j[s][:, t, :], ACT.Copy,
                                               scale=picks[:, 2, bass.ds(i * 16 + (4 * s + t), 1)])
                ins.then_inc(hot_gated, 1)

            act.wait_ge(picks_out, 2)
            for s in range(4):
                send_keys(None, s)
            hot_gates(0, 0)
            hot_gates(0, 1)
            a_half(NKEYS // 4 - 1, 3)
            a_gelu(NKEYS // 4 - 1, 3)
            hot_gates(0, 2)
            hot_gates(0, 3)
            for s in range(4):
                send_keys(0, s)
            with act.Fori(1, SEQ // 16 - 1) as i:
                for s in range(4):
                    hot_gates(i, s)
                    send_keys(i, s)
            for s in range(4):
                hot_gates(SEQ // 16 - 1, s)

            def c_part(i, c):
                act.wait_ge(used, i * 4 + (V0 + 2 * c - 2))
                nc.scalar.activation(c_hi[:, c, :], act_all[:, bass.ds(i * 2 + c, 1), :].rearrange("p a n -> p (a n)"),
                                     ACT.Copy).then_inc(ch_done, 1)

            act.wait_ge(g_used, 64)
            with act.Fori(0, NKEYS // 2) as i:
                for p in range(4):
                    if p % 2 == 0:
                        c_part(i, p // 2)
                    split_hi(V0 + p, i)

        @block.vector
        def _(dve):
            V = nc.vector
            link = linked(dve, dve_step)

            def split_lo(n, i, width=PIECE, per=4):
                dve.wait_ge(hi_done, i * per + (n + 1))
                V.tensor_tensor(lo[:, n % SPL, 0:width], raw[:, n % RAW, 0:width],
                                hi[:, n % SPL, 0:width].bitcast(F32), ALU.subtract).then_inc(lo_done, 1)

            def mean(a, n, width):
                return V.tensor_scalar(st[:, a:a + n], st[:, a:a + n], 1.0 / width, EPS, ALU.mult, ALU.add)

            def inverse(k, a, n):
                dve.wait_ge(root, k)
                link(V.reciprocal(rr[:, a:a + n], rs[:, a:a + n]))

            def turn_lo(s, a, e):
                to_hi, to_lo = splits[s][2:4]
                for k in range(2 * a, 2 * e):
                    fill = fills_before[s] + k // 2
                    dve.wait_ge(t_hi, 2 * (fill + 1))
                    V.scalar_tensor_tensor(to_lo[:, k, :], fill_bank(s, fill)[:, (k % 2) * SEQ:(k % 2 + 1) * SEQ],
                                           gain_of(s, k), to_hi[:, k, :].bitcast(F32),
                                           ALU.mult, ALU.subtract).then_inc(t_lo, 1)

            def square_sum(junk, v, k):
                link(V.tensor_tensor_reduce(junk, v, v, 1.0, 0.0, ALU.mult, ALU.add, st[:, k:k + 1]))

            def qk_stats(s):
                if s < 2:
                    dve.wait_ge(sq_done, 2 + s)
                    k = S_Q + s * HEADS
                    link(V.tensor_reduce(st[:, k:k + HEADS], sq_q[:, s], AX.X, ALU.add))
                else:
                    b = s - 2
                    dve.wait_ge(sq_done, 4 + b)
                    k = S_K + b * HEADS
                    link(V.tensor_reduce(st[:, k:k + HEADS], sq_k[:, b], AX.X, ALU.add))
                    square_sum(sq_k[:, b, 0, 0:ROPE], lat[:, b, LAT - ROPE:LAT], S_KR + b)
                    link(V.tensor_scalar(st[:, k:k + HEADS], st[:, k:k + HEADS], st[:, S_KR + b:S_KR + b + 1], None, ALU.add))
                if s == 3:
                    mean(S_Q, 32, QK).then_inc(stat, 1)

            def score_max(b):
                nk = P * (b + 1)
                for f in range(4):
                    dve.wait_ge(s_ready, 4 * b + f + 1)
                    h = 4 * (f % 2) + f // 2
                    link(V.tensor_reduce(nmax[:, 0, b, h:h + 3:2],
                                         bank[4 + f][:, :].rearrange("p (h n) -> p h n", h=2)[:, :, 0:nk], AX.X, ALU.max))
                V.tensor_scalar(nmax[:, 1, b, :], nmax[:, 0, b, :], -1.0, None, ALU.mult).then_inc(s_max, 1)

            def softmax_scale(b):
                nk = P * (b + 1)
                dve.wait_ge(s_exp, b + 1)
                link(V.reciprocal(sums[:, 1, b, :], sums[:, 0, b, :]))
                V.tensor_tensor(prob[:, :, 0:nk], prob[:, :, 0:nk], bc(sums[:, 1, b, :], nk), ALU.mult).then_inc(p_ready, 1)

            def pv_split(b):
                for f in range(2):
                    dve.wait_ge(pv_hi, 2 * b + f + 1)
                    at_ = (slice(None), slice(4 * f, 4 * f + 4), slice(b * P, (b + 1) * P))
                    V.tensor_tensor(mix_lo[at_], bank[pv_bank(b, f)][:, :].rearrange("p (h n) -> p h n", h=4),
                                    mix_hi[at_].bitcast(F32), ALU.subtract).then_inc(pv_lo, 1)

            def gmlp_gate(h0):
                for b, h in ((0, h0), (0, h0 + 1), (1, h0), (1, h0 + 1)):
                    dve.wait_ge(sv_ready, 2 * b + h // 4 + 1)
                    u = zu[:, b, h * P:(h + 1) * P]
                    V.scalar_tensor_tensor(u, bank[sv_bank(b, h // 4)][:, (h % 4) * P:(h % 4 + 1) * P],
                                           cols[:, C_BS + h:C_BS + h + 1], u, ALU.add, ALU.mult).then_inc(gm_ready, 1)

            def residual(m):
                dve.wait_ge(used, FIRST_OUT + 8 * (m + 1))
                for b in range(NB):
                    xc = x[:, b, m * COLG:(m + 1) * COLG]
                    ins = V.tensor_tensor(xc, bank[2 * ((13 + m) % 2) + b][:, :], xc, ALU.add)
                ins.then_inc(x2_ready, 1)

            dve.wait_ge(cols_in, 16)
            V.tensor_scalar(gq[:, :], cols[:, C_QG:C_QG + 1], QSCALE, None, ALU.mult).then_inc(gq_set, 1)
            for n in range(WQ0):
                g, what, k, pieces, c = group_of(n)
                if n < KD // 2:
                    turn_lo(0, n, n + 1)
                split_lo(n, 0, KP * c)
                if n == 4:
                    for x_part in x_in:
                        dve.wait_ge(x_part, 16)
                    square_sum(sq_x[:, 0, :], x[:, 0, :], S_X)
                if n == 5:
                    dve.wait_ge(sq_done, 1)
                    mean(S_X, 2, D).then_inc(stat, 1)
                if n == 7:
                    dve.wait_ge(root, 1)
                    V.reciprocal(rr[:, S_X:S_X + 2], rs[:, S_X:S_X + 2]).then_inc(x_rms, 1)
                if n == 11:
                    dve.wait_ge(acc_out, 1)
                    for b in range(NB):
                        square_sum(sq_x[:, 0, 0:Q_RANK], lat[:, b, 0:Q_RANK], S_LAT + b)
                if n == 17:
                    dve.wait_ge(acc_out, 2)
                    for b in range(NB):
                        square_sum(sq_x[:, 0, 0:KV_RANK], lat[:, b, Q_RANK:Q_RANK + KV_RANK], S_LAT + 2 + b)
                    link(mean(S_LAT, 2, Q_RANK))
                    mean(S_LAT + 2, 2, KV_RANK).then_inc(stat, 1)
                if n == 18:
                    inverse(2, S_LAT, 4)
                    for b in range(NB):
                        for a, e, m in ((0, Q_RANK, 0), (Q_RANK, Q_RANK + KV_RANK, 2)):
                            k_ = S_LAT + m + b
                            V.tensor_scalar(lat[:, b, a:e], lat[:, b, a:e], rr[:, k_:k_ + 1], None, ALU.mult).then_inc(scaled, 1)
                if n == 22:
                    turn_lo(1, 0, 3)
                if n in (33, 34, 36, 37):
                    qk_stats((33, 34, 36, 37).index(n))
                if n == 38:
                    dve.wait_ge(root, 3)
                    V.reciprocal(rr[:, S_Q:S_Q + 32], rs[:, S_Q:S_Q + 32]).then_inc(k_norm, 1)
                    dve.wait_ge(k_norm, 1)
                if n in (39, 40):
                    b = n - 39
                    V.tensor_tensor(q[:, b], q[:, b], bc(rr[:, S_Q + b * HEADS:S_Q + (b + 1) * HEADS], QK), ALU.mult).then_inc(q_norm, 1)
                    dve.wait_ge(q_norm, b + 1)
                if n in (41, 43):
                    b = (n - 41) // 2
                    dve.wait_ge(rows_in, 32)
                    link(V.tensor_tensor(qr[:, b], q[:, b, :, NOPE:QK], over_heads(rows[:, R_Q:R_Q + ROPE]), ALU.mult))
                    rotate(V, link, qr[:, b], b, tmp_q, q_ready, sums=False)
                if n in (42, 44):
                    b = (n - 42) // 2
                    rotate(V, link, qr[:, b], b, tmp_q, q_ready, products=False)
                    dve.wait_ge(q_ready, b + 1)
                if n in (45, 46):
                    b = n - 45
                    dve.wait_ge(acc_out, 11)
                    square_sum(tmp_q, zv[:, b, :], S_V + b)
                    if b:
                        mean(S_V, 2, GW).then_inc(stat, 1)
                if n == 47:
                    score_max(0)
                if n == 48:
                    inverse(4, S_V, 2)
                if n == 49:
                    softmax_scale(0)
                if n in (50, 53):
                    b = (n - 50) // 3
                    V.scalar_tensor_tensor(zv[:, b, :], zv[:, b, :], rr[:, S_V + b:S_V + b + 1], rows[:, R_V:R_V + GW],
                                           ALU.mult, ALU.mult).then_inc(v_ready, 1)
                if n == 51:
                    pv_split(0)
                if n == 52:
                    score_max(1)
                if n == 54:
                    softmax_scale(1)
                if n == 57:
                    pv_split(1)
                if FIRST_OUT < n <= FIRST_OUT + 4:
                    dve.wait_ge(acc_out, 13)
                    gmlp_gate(2 * (n - FIRST_OUT - 1))
                if FIRST_OUT + 3 <= n < FIRST_OUT + 7:
                    turn_lo(2, n - FIRST_OUT - 3, n - FIRST_OUT - 2)
                if k == 0 and g > 13:
                    residual(g - 14)
                if k == 3 and g > 13:
                    turn_lo(3, 2 * (g - 14), 2 * (g - 13))

            def take_scores(i, c):
                dve.wait_ge(sc_ready, i * 2 + (c + 1))
                for b in range(NB):
                    ins = V.tensor_scalar(score.rearrange("p (b m) -> p b m", b=NB)[:, b, bass.ds(i * 2 * NKEYS + c * NKEYS, NKEYS)],
                                          bank[4 + c][:, b * NKEYS:(b + 1) * NKEYS], rr[:, S_X2 + b:S_X2 + b + 1], None, ALU.mult)
                ins.then_inc(sc_out, 1)

            def wq_body(i, norm=False):
                quarter = bass.ds(i * 4 - 4, 4)
                for p in range(4):
                    split_lo(WQ0 + p, i)
                    if p == 0:
                        take_scores(i - 1, 0)
                    if p == 2:
                        take_scores(i - 1, 1)
                    if p == 0 and norm:
                        V.tensor_tensor(full[:, :, :], htw_hi[:, quarter, :].bitcast(F32),
                                        htw_lo[:, quarter, :].bitcast(F32), ALU.add).then_inc(full_sum, 1)
                    if p == 1 and norm:
                        dve.wait_ge(full_sum, i * 1)
                        V.tensor_tensor(full[:, :, :], full[:, :, :],
                                        bank[6][:, 0:SEQ].unsqueeze(1).to_broadcast((P, 4, SEQ)), ALU.mult).then_inc(full_norm, 1)
                    if p == 3 and norm:
                        dve.wait_ge(n_hi, i * 1)
                        V.tensor_tensor(ht_lo[:, quarter, :], full[:, :, :], ht_hi[:, quarter, :].bitcast(F32),
                                        ALU.subtract).then_inc(n_lo, 1)
                        dve.wait_ge(n_lo, i * 1)

            def a_add(i, c):
                dve.wait_ge(a_rest, i * 4 + (c + 1))
                V.tensor_tensor(a_part[:, c % 2, :], bank[c % 2][:, 0:SEQ], a_part[:, c % 2, :], ALU.add).then_inc(a_sum, 1)

            def u_split(i, p, first=False):
                split_lo(U0 + p, i, per=8)
                if p % 2 == 0 and (p or not first):
                    a_add(i - (p < 2), (p // 2 - 1) % 4)

            def topk_body(i):
                dve.sem_clear(dve_topk)
                link = linked(dve, dve_topk)

                def eight(out8, idx, src, values):
                    link(V.max(out8, src))
                    link(V.max_index(idx, out8, values))

                def half(a, r):
                    src = sw[:, a, :] if r == 0 else sw2
                    eight(sv[:, a * TOPK + 8 * r:a * TOPK + 8 * r + 8], i8[:, a * TOPK + 8 * r:a * TOPK + 8 * r + 8], src, src)

                def rest(a):
                    link(V.match_replace(sw2, sv[:, a * TOPK:a * TOPK + 8], sw[:, a, :], LOWEST))

                for p in range(8):
                    u_split(i, p)
                    if p == 0:
                        link(V.tensor_copy(sw.rearrange("p a n -> p (a n)"), score[:, bass.ds((i - 1) * 2 * NKEYS, 2 * NKEYS)]))
                        half(0, 0)
                    if p == 1:
                        rest(0)
                        half(0, 1)
                    if p == 2:
                        half(1, 0)
                        rest(1)
                    if p == 3:
                        half(1, 1)
                    if p == 4:
                        link(V.tensor_tensor(cand.rearrange("p (a n) -> p a n", a=TOPK), bc(sv[:, 0:TOPK], TOPK),
                                             sv[:, TOPK:2 * TOPK].unsqueeze(1).to_broadcast((P, TOPK, TOPK)), ALU.add))
                        eight(tops[:, 0:8], pos[:, 0:8], cand, cand)
                    if p == 5:
                        link(V.match_replace(cand2, tops[:, 0:8], cand, LOWEST))
                        eight(tops[:, 8:16], pos[:, 8:16], cand2, cand2)
                    if p == 6:
                        V.tensor_copy(all_top[:, bass.ds((i - 1) * TOPK, TOPK)], tops)
                        V.tensor_copy(all_pos[:, bass.ds((i - 1) * TOPK, TOPK)], pos)
                        link(V.tensor_copy(all_id[:, bass.ds((i - 1) * 2 * TOPK, 2 * TOPK)], i8))

            def pick_body(i):
                r = i - 18
                dve.sem_clear(dve_pick)
                link = linked(dve, dve_pick)
                hot4 = hot.rearrange("p (g k m) -> p g k m", g=4, k=TOPK)
                for p in range(8):
                    u_split(i, p)
                    a, s = p // 4, p % 4
                    where = posf[:, bass.ds(r * 64 + a * NTOP, 64)].rearrange("p (g k) -> p g k", g=4)
                    ids = idf[:, bass.ds(r * 128, 128)].rearrange("p (g a m) -> p g a m", g=4, a=2)[:, :, a, :]
                    full = (P, 4, TOPK, TOPK)
                    if s == 0:
                        link(V.tensor_tensor(hot4, where.unsqueeze(3).to_broadcast(full),
                                             iota[:, 0:TOPK].unsqueeze(1).unsqueeze(1).to_broadcast(full), ALU.is_equal))
                    if s == 1:
                        link(V.tensor_tensor(hot4, hot4, ids.unsqueeze(2).to_broadcast(full), ALU.mult))
                    if s == 2:
                        link(V.tensor_reduce(key_of[:, bass.ds(r * 64 + a * NTOP, 64)].rearrange("p (g k) -> p g k", g=4),
                                             hot4, AX.X, ALU.add))

            def plain_body(i):
                for p in range(8):
                    u_split(i, p)

            for p in range(4):
                split_lo(WQ0 + p, 0)
                if p == 0:
                    residual(3)
                if p == 1:
                    turn_lo(3, 6, 8)
                if p == 2:
                    dve.wait_ge(x2_sq, 4)
                    link(V.tensor_reduce(st[:, S_X2:S_X2 + 2], st[:, S_PART:S_PART + 8].rearrange("p (b m) -> p b m", b=NB), AX.X, ALU.add))
                    mean(S_X2, 2, D).then_inc(stat, 1)
                    dve.wait_ge(iota_set, 1)
                    V.tensor_scalar(norm_rows[:, 0, :], iota[:, :], 0.0, None, ALU.is_ge).then_inc(diag_set, 1)
                if p == 3:
                    inverse(5, S_X2, 2)
                    for b in range(NB):
                        V.tensor_scalar(norm_rows[:, 1 + b, :], ident[:, :], rr[:, S_X2 + b:S_X2 + b + 1], None, ALU.mult).then_inc(diag_set, 1)
            dve.wait_ge(rms_row, 1)
            with dve.Fori(1, 5) as i:
                wq_body(i, True)
            with dve.Fori(5, HP // 2) as i:
                wq_body(i)
            for p in range(8):
                u_split(0, p, True)
                if p == 0:
                    take_scores(HP // 2 - 1, 0)
                if p == 2:
                    take_scores(HP // 2 - 1, 1)
            dve.wait_ge(sc_out, HP)
            with dve.Fori(1, 17) as i:
                topk_body(i)
            dve.wait_ge(iota_set, 1)
            late = linked(dve, dve_late)
            for p in range(8):
                u_split(17, p)
                if p == 0:
                    late(V.tensor_scalar(posu[:, 0:NTOP], all_pos, 4, None, ALU.logical_shift_right))
                    late(V.tensor_scalar(posu[:, NTOP:2 * NTOP], all_pos, TOPK - 1, None, ALU.bitwise_and))
                if p == 1:
                    late(V.tensor_copy(posf, posu))
                    late(V.tensor_copy(idf, all_id))
            with dve.Fori(18, 22) as i:
                pick_body(i)
            top3 = all_top.rearrange("p (g k) -> p g k", k=TOPK)
            gate3 = gate.rearrange("p (g k) -> p g k", k=TOPK)
            for p in range(8):
                u_split(22, p)
                if p == 0:
                    V.tensor_tensor(gate3, top3, top3[:, :, 0:1].to_broadcast((P, NB * HEADS, TOPK)), ALU.subtract).then_inc(gate_in, 1)
            for p in range(8):
                u_split(23, p)
                if p == 4:
                    dve.wait_ge(gate_exp, 1)
                    late(V.tensor_reduce(smx[:, 0:NB * HEADS], gate3, AX.X, ALU.add))
                    late(V.reciprocal(smx[:, NB * HEADS:2 * NB * HEADS], smx[:, 0:NB * HEADS]))
                    V.tensor_tensor(gate3, gate3, bc(smx[:, NB * HEADS:2 * NB * HEADS], TOPK), ALU.mult).then_inc(picks_ready, 1)
            with dve.Fori(24, NKEYS // 4) as i:
                plain_body(i)

            def hot_rows(i, s, first=False):
                if not first:
                    dve.wait_ge(g_ready, i * 4 + (s - 3))
                t0 = i * 16 + 4 * s

                def hot(out, a, n):
                    keys = picks[:, a, bass.ds(t0, n)]
                    return V.tensor_tensor(out, iota[:, :].unsqueeze(1).to_broadcast((P, n, P)), bc(keys, P), ALU.is_equal)
                hot(one_j[s], 1, 4).then_inc(hot_j, 1)
                hot(one_i[s][:, 0:2, :], 0, 2).then_inc(hot_i, 1)

            def gate_rows(i, s):
                dve.wait_ge(g_ready, i * 4 + (s + 1))
                a4 = act_all[:, :, bass.ds(i * 16 + 4 * s, 4)].rearrange("p j t -> p t j")
                V.tensor_tensor(a4, bank[4 + s][:, :].rearrange("p (t j) -> p t j", t=4), a4, ALU.mult).then_inc(g_used, 1)

            dve.wait_ge(picks_out, 2)
            hot_rows(0, 0, True)
            hot_rows(0, 1, True)
            a_add(NKEYS // 4 - 1, 3)
            hot_rows(0, 2, True)
            dve.wait_ge(a_out, NKEYS)
            gate_rows(0, 0)
            hot_rows(0, 3, True)
            gate_rows(0, 1)
            with dve.Fori(1, SEQ // 16) as i:
                for s in range(4):
                    hot_rows(i, s)
                    if s < 2:
                        gate_rows(i - 1, s + 2)
                    else:
                        gate_rows(i, s - 2)
            gate_rows(SEQ // 16 - 1, 2)
            gate_rows(SEQ // 16 - 1, 3)
            dve.wait_ge(g_used, 64)

            with dve.Fori(0, NKEYS // 2) as i:
                for p in range(4):
                    if p % 2 == 0:
                        c = p // 2
                        dve.wait_ge(ch_done, i * 2 + (c + 1))
                        V.tensor_tensor(c_lo[:, c, :], act_all[:, bass.ds(i * 2 + c, 1), :].rearrange("p a n -> p (a n)"),
                                        c_hi[:, c, :].bitcast(F32), ALU.subtract).then_inc(cl_done, 1)
                    split_lo(V0 + p, i)
            for p in range(4):
                n = X0 + p
                dve.wait_ge(used, X0 - 1 + p // 2)
                dve.wait_ge(raw_in[n % RAW], 16 * (n // RAW + 1))
                for m in range(2):
                    r = raw[:, n % RAW, m * COLG:(m + 1) * COLG]
                    V.tensor_tensor(r, bank[4 * (p % 2) + 2 * (p // 2) + m][:, :], r, ALU.add).then_inc(y_ready, 1)

        @block.tensor
        def _(pe):
            MM = nc.tensor.matmul

            def turn(s, a, e):
                src = splits[s][0]
                for f in range(a, e):
                    fill = fills_before[s] + f
                    if s == 2:
                        pe.wait_ge(t_lo, 2 * (fill - 1))
                        pe.wait_ge(acc_out, 13)
                    elif fill >= 4:
                        pe.wait_ge(t_lo, 2 * (fill - 3))
                    for k in (2 * f, 2 * f + 1):
                        for b in range(NB):
                            m = nc.tensor.transpose(fill_bank(s, fill)[:, (k % 2) * SEQ + b * P:(k % 2) * SEQ + (b + 1) * P],
                                                    src(k, b), ident[:, :])
                    m.then_inc(turned, 1)

            def column_piece(n, i, outs, a_hi, a_lo, c, kk, first, last, skip=False):
                s = n % SPL
                pe.wait_ge(hi_done, i * 4 + (n + 1))
                parts = [(k, b, m) for k in range(kk) for b in range(NB) for m in range(len(outs[0]))]

                def w(part, k, m):
                    a = k * c + m * COLG
                    return part[:, s, a:a + min(c, COLG)]

                for k, b, m in parts:
                    MM(outs[b][m], a_hi(k, b), w(hi, k, m), start=first and k == 0, stop=False, skip_group_check=skip)
                for k, b, m in parts:
                    MM(outs[b][m], a_lo(k, b), w(hi, k, m), start=False, stop=False, skip_group_check=skip)
                pe.wait_ge(lo_done, i * 4 + (n + 1))
                for k, b, m in parts:
                    ins = MM(outs[b][m], a_hi(k, b), w(lo, k, m), start=False, stop=last and k == kk - 1, skip_group_check=skip)
                ins.then_inc(used, 1)

            def query_piece(n, i, out, half):
                s = n % SPL
                pe.wait_ge(hi_done, i * 4 + (n + 1))
                for k in range(8):
                    w = hi[:, s, k * P:(k + 1) * P]
                    MM(out, w, htw_hi[:, 8 * half + k, :], start=(half == 0 and k == 0), stop=False)
                    MM(out, w, htw_lo[:, 8 * half + k, :], start=False, stop=False)
                pe.wait_ge(lo_done, i * 4 + (n + 1))
                for k in range(8):
                    ins = MM(out, lo[:, s, k * P:(k + 1) * P], htw_hi[:, 8 * half + k, :], start=False, stop=(half == 1 and k == 7))
                ins.then_inc(used, 1)

            def expert_piece(n, i, out, half):
                s = n % SPL
                pe.wait_ge(hi_done, i * 8 + (n + 1))
                for k in range(8):
                    MM(out[:, :], hi[:, s, k * P:(k + 1) * P], ht[:, 8 * half + k, :, :].rearrange("p a n -> p (a n)"),
                       start=(half == 0 and k == 0), stop=False, skip_group_check=True)
                pe.wait_ge(lo_done, i * 8 + (n + 1))
                for k in range(8):
                    ins = MM(out[:, 0:SEQ], lo[:, s, k * P:(k + 1) * P], ht_hi[:, 8 * half + k, :],
                             start=False, stop=(half == 1 and k == 7), skip_group_check=True)
                ins.then_inc(used, 1)

            def turn_qk(a, e):
                for j in range(a, e):
                    if j >= 4:
                        pe.wait_ge(qk_out, j - 3)
                    if j == 0:
                        pe.wait_ge(q_norm, 2)
                    if j == 4:
                        pe.wait_ge(k_ready, 2)
                    if j == 8:
                        pe.wait_ge(q_ready, 2)
                    f = QK_ORDER[j]
                    h = f % 6
                    for r in range(2):
                        for b in range(NB):
                            if h < 4:
                                src = q[:, b, 2 * h + r, 0:NOPE] if f < 6 else kv[:, b, 2 * h + r, 0:NOPE]
                            else:
                                a2 = 2 * (2 * (h - 4) + r)
                                src = (qr if f < 6 else kr)[:, b, a2:a2 + 2, :].rearrange("p h n -> p (h n)")
                            m = nc.tensor.transpose(bank[4 + j % 4][:, r * SEQ + b * P:r * SEQ + (b + 1) * P], src, ident[:, :])
                    m.then_inc(qk_turned, 1)

            def scores(b):
                nk = P * (b + 1)
                if b == 0:
                    pe.wait_ge(qk_out, 12)
                    pe.wait_ge(mask_set, 1)
                else:
                    pe.wait_ge(p_out, 2)
                    pe.wait_ge(pv_lo, 2)
                for h in (0, 2, 4, 6, 1, 3, 5, 7):
                    f, a = score_at(h)
                    o = bank[f][:, a:a + nk]
                    r = slice(ROPE * (h % 2), ROPE * (h % 2) + ROPE)
                    MM(o, qt[:, h, b * P:(b + 1) * P], kt[:, h, 0:nk], start=True, stop=False)
                    MM(o, qtr[r, h // 2, b * P:(b + 1) * P], ktr[r, h // 2, 0:nk], start=False, stop=False)
                    m = MM(o, mrow[:, 0:P], mrow[:, P + SEQ - nk:P + SEQ], start=False, stop=True)
                    if a:
                        m.then_inc(s_ready, 1)

            def turn_p(b):
                pe.wait_ge(p_ready, b + 1)
                for h in range(HEADS):
                    for k in range(b + 1):
                        per = 4 // (b + 1)
                        f = h // per
                        a = ((h % per) * (b + 1) + k) * P
                        m = nc.tensor.transpose(bank[4 + f][:, a:a + P], prob[:, h, k * P:(k + 1) * P], ident[:, :])
                    if h % per == per - 1:
                        m.then_inc(p_turned, 1)

            def pv(b):
                pe.wait_ge(p_out, 2 if b == 0 else 6)
                for h in range(HEADS):
                    for k in range(b + 1):
                        m = MM(bank[pv_bank(b, h // 4)][:, (h % 4) * P:(h % 4 + 1) * P], kv[:, k, h, NOPE:2 * NOPE],
                               prt[:, h, k, :], start=(k == 0), stop=(k == b))
                    if h % 4 == 3:
                        m.then_inc(pv_ready, 1)

            def spatial(b):
                pe.wait_ge(v_ready, b + 1)
                if b == 0:
                    pe.wait_ge(wst_masked, 1)
                else:
                    pe.wait_ge(pv_lo, 4)
                for h in range(HEADS):
                    m = MM(bank[sv_bank(b, h // 4)][:, (h % 4) * P:(h % 4 + 1) * P], wst[:, h, :],
                           zv[:, b, h * P:(h + 1) * P], start=True, stop=True)
                    if h % 4 == 3:
                        m.then_inc(sv_ready, 1)

            pe.wait_ge(ident_set, 1)
            x_load = [next(c for c, e in enumerate(X_CUTS[1:]) if (f + 1) * SEQ <= e) for f in range(KD // 2)]
            for n in range(WQ0):
                g, what, k, pieces, c = group_of(n)
                for f in (0, 1) if n == 0 else (n + 1,) if n + 1 < KD // 2 else ():
                    pe.wait_ge(x_in[x_load[f]], 16)
                    turn(0, f, f + 1)
                if k == 0:
                    if 2 <= g < 15:
                        pe.wait_ge(acc_out, g - 1)
                    if g >= 15:
                        pe.wait_ge(x2_ready, g - 14)
                    if what in ("q", "kv"):
                        pe.wait_ge(t_lo, 2 * fills_before[2])
                    if what == "out":
                        pe.wait_ge(pv_lo, 4)
                if what == "cq":
                    pe.wait_ge(t_lo, 2 * (k + 1))
                if what == "out" and k >= 4:
                    pe.wait_ge(t_lo, 2 * (fills_before[2] + k - 3))
                lo_k = KP * k
                if what == "q":
                    src = (ct_hi, ct_lo, lo_k)
                elif what == "kv":
                    src = (ct_hi, ct_lo, 4)
                elif what == "out":
                    src = (mix_hi, mix_lo, lo_k) if k < 4 else (ht_hi, ht_lo, lo_k - HEADS)
                else:
                    src = (ht_hi, ht_lo, lo_k)
                s_hi, s_lo, k0 = src
                column_piece(n, 0, [[bank[2 * (g % 2) + b][:, 0:c]] for b in range(NB)],
                             lambda kk, b: s_hi[:, k0 + kk, b * P:(b + 1) * P],
                             lambda kk, b: s_lo[:, k0 + kk, b * P:(b + 1) * P],
                             c, KP, k == 0, k == pieces - 1)
                if n == 20:
                    pe.wait_ge(scaled, 4)
                    turn(1, 0, 3)
                if n in (42, 43, 44):
                    turn_qk(4 * (n - 42), 4 * (n - 41))
                if n == 46:
                    scores(0)
                if n == 49:
                    turn_p(0)
                if n == 50:
                    pv(0)
                if n == 51:
                    scores(1)
                if n == 54:
                    turn_p(1)
                if n == 56:
                    pv(1)
                    spatial(0)
                if n == FIRST_OUT:
                    spatial(1)
                if FIRST_OUT + 2 <= n < FIRST_OUT + 6:
                    f = n - FIRST_OUT - 2
                    pe.wait_ge(gm_ready, 4 * (f + 1))
                    turn(2, f, f + 1)
                if k == 2 and g > 13:
                    pe.wait_ge(x2_ready, g - 13)
                    turn(3, 2 * (g - 14), 2 * (g - 13))

            def key_scores(i, c, first=False):
                pe.wait_ge(q_out, i * 2 + (c + 1))
                if not first:
                    pe.wait_ge(sc_out, i * 2 + (c - 1))
                for b in range(NB):
                    m = MM(bank[4 + c][:, b * P:(b + 1) * P], qp[:, c, b * P:(b + 1) * P],
                           subkeys[:, bass.ds(i * 2 + c, 1), :].rearrange("p a n -> p (a n)"), start=True, stop=True)
                m.then_inc(sc_ready, 1)

            def wq_body(i, first, second=False):
                for p in range(4):
                    if p < 2 and not first:
                        pe.wait_ge(q_out, i * 2 + (p - 1))
                    if first and p == 0:
                        pe.wait_ge(x2_ready, 3)
                        pe.wait_ge(t_lo, 2 * (fills_before[3] + 6))
                    if first and p == 2:
                        pe.wait_ge(t_lo, 2 * fills_before[4])
                    query_piece(WQ0 + p, i, bank[2 + p % 2][:, 0:SEQ], p // 2)
                    if first and p == 0:
                        pe.wait_ge(x2_ready, 4)
                        turn(3, 6, 8)
                    if p == 1 and not first:
                        key_scores(i - 1, 1, second)
                    if p == 3:
                        if first:
                            pe.wait_ge(diag_set, 3)
                            MM(bank[6][:, 0:SEQ], norm_rows[:, 0, :], norm_rows[:, 1:3, :].rearrange("p b n -> p (b n)"),
                               start=True, stop=True).then_inc(rms_row, 1)
                            pe.wait_ge(sub_in, 16)
                        key_scores(i, 0, first)

            def u_body(i, first=False):
                for p in range(8):
                    c = p // 2
                    if p % 2 == 0 and not (first and c < 2):
                        pe.wait_ge(a_sum, i * 4 + (c - 1))
                    if first and p == 0:
                        pe.wait_ge(n_lo, 4)
                    expert_piece(U0 + p, i, bank[c % 2], p % 2)
                    if p == 1 and first:
                        key_scores(HP // 2 - 1, 1)

            wq_body(0, True)
            wq_body(1, False, True)
            with pe.Fori(2, HP // 2) as i:
                wq_body(i, False)
            u_body(0, True)
            with pe.Fori(1, 24) as i:
                u_body(i)
            pe.wait_ge(picks_ready, 1)
            for a, src in enumerate((key_of[:, 0:NTOP], key_of[:, NTOP:2 * NTOP], gate)):
                for b in range(NB):
                    o = bank[4 + a // 2][:, (a % 2) * SEQ + b * P:(a % 2) * SEQ + (b + 1) * P]
                    m = nc.tensor.transpose(o, src[:, b * P:(b + 1) * P], ident[:, :])
            m.then_inc(picks_turned, 1)
            with pe.Fori(24, NKEYS // 4) as i:
                u_body(i)

            def gates(i, s, first=False):
                pe.wait_ge(hot_gated, i * 4 + (s + 1))
                pe.wait_ge(hot_i, i * 4 + (s + 1))
                pe.wait_ge(hot_i2, i * 4 + (s + 1))
                if not first:
                    pe.wait_ge(g_used, i * 4 + (s - 3))
                for t in range(4):
                    m = MM(bank[4 + s][:, t * P:(t + 1) * P], one_i[s][:, t, :], one_j[s][:, t, :], start=True, stop=True)
                m.then_inc(g_ready, 1)

            for s in range(4):
                gates(0, s, True)
            with pe.Fori(1, SEQ // 16) as i:
                for s in range(4):
                    gates(i, s)

            def v_body(i, first=False, last=False):
                for p in range(4):
                    c, h = p // 2, p % 2
                    if h == 0:
                        pe.wait_ge(cl_done, i * 2 + (c + 1))
                    column_piece(V0 + p, i, [[bank[4 * b + 2 * h + m][:, :] for m in range(2)] for b in range(NB)],
                                 lambda k, b: c_hi[:, c, b * P:(b + 1) * P], lambda k, b: c_lo[:, c, b * P:(b + 1) * P],
                                 PIECE, 1, first and c == 0, last and c == 1, skip=True)

            v_body(0, first=True)
            with pe.Fori(1, NKEYS // 2 - 1) as i:
                v_body(i)
            v_body(NKEYS // 2 - 1, last=True)


def score_at(h):
    return 4 + 2 * (h % 2) + h // 4, SEQ * (h // 2 % 2)


def pv_bank(b, f):
    return (6 if b == 0 else 4) + f


def sv_bank(b, f):
    return (6 if b == 0 else 4) + f


def column_pieces(np, w, groups, kp=KP):
    out = []
    for a, c in groups:
        m = w[:, a:a + c].reshape(-1, kp, P, c)
        out.append(np.ascontiguousarray(m.transpose(0, 2, 1, 3)).reshape(-1, P, kp * c))
    return np.concatenate(out)


def row_pieces(np, w):
    m = w.reshape(2, 8, P, -1, 2, P)
    return np.ascontiguousarray(m.transpose(3, 0, 4, 2, 1, 5)).reshape(-1, P, 8 * P)


def kernel(x, norm_mix_g, w_in, gmlp_vnorm_g, gmlp_ws, gmlp_bs, mla_qnorm_g, mla_w_uq,
           mla_kvnorm_g, mla_w_ukv, mla_qk_q_g, mla_qk_k_g, w_out, norm_ffn_g,
           peer_w_q, peer_subkeys, peer_u, peer_v):
    import numpy as np
    import concourse.bacc as bacc
    from concourse.bass_utils import run_bass_kernel_spmd

    def col(g):
        return g.reshape(-1, P).T

    w = w_in[0]
    two = [(k * COLG, COLG) for k in range(2)]
    wo = np.concatenate([w_out[0, GW:], w_out[0, :GW]])
    pos = np.arange(SEQ, dtype=np.float32)
    inv = (np.float32(10000.0) ** (-np.arange(0, ROPE, 2, dtype=np.float32) / np.float32(ROPE))).astype(np.float32)
    ang = pos[:, None] * inv[None, :]
    rope = np.stack([np.cos(ang), np.sin(ang)], 1).astype(np.float32)
    arrays = {
        "x": x.reshape(SEQ, D),
        "w_cq": column_pieces(np, w, [(2 * GW, Q_RANK)]),
        "w_ckv": column_pieces(np, w, [(2 * GW + Q_RANK, KV_RANK + ROPE)]),
        "w_zv": column_pieces(np, w, [(GW + a, c) for a, c in two]),
        "w_zu": column_pieces(np, w, two),
        "w_out": column_pieces(np, wo, [(k * COLG, COLG) for k in range(4)]),
        "w_kv": column_pieces(np, mla_w_ukv[0], [(k * COLG, COLG) for k in range(4)]),
        "w_uq": column_pieces(np, mla_w_uq[0], [(k * COLG, COLG) for k in range(3)]),
        "w_pq": row_pieces(np, peer_w_q[0]),
        "peer_u": np.ascontiguousarray(
            peer_u[0].reshape(P, NKEYS, 2, 8, P).transpose(1, 2, 4, 3, 0)).reshape(-1, P, PIECE),
        "peer_v": np.ascontiguousarray(
            peer_v[0].reshape(P, NKEYS, 2, PIECE).transpose(1, 2, 0, 3)).reshape(-1, P, PIECE),
        "subkeys": np.ascontiguousarray(peer_subkeys[0].reshape(HP, NKEYS, P).transpose(2, 0, 1)),
        "ws": np.ascontiguousarray(gmlp_ws[0].transpose(2, 0, 1)),
        "rope": np.ascontiguousarray(rope.reshape(NB, P, 2, ROPE // 2).transpose(1, 0, 2, 3)),
        "cols": np.ascontiguousarray(np.concatenate(
            [col(norm_mix_g[0]), col(norm_ffn_g[0]), col(mla_qnorm_g[0]), col(mla_kvnorm_g[0]),
             col(mla_qk_q_g[0, :NOPE]), col(mla_qk_k_g[0, :NOPE]), gmlp_bs[0].T], axis=1)),
        "rows": np.concatenate([gmlp_vnorm_g[0], mla_qk_q_g[0, NOPE:], mla_qk_k_g[0, NOPE:]]).reshape(1, NROWS),
    }
    nc = bacc.Bacc("TRN2", target_bir_lowering=False, num_devices=1, dynamic_dma_scratch_size=4096)
    d = {}
    for name, a in arrays.items():
        d[name] = nc.dram_tensor(f"in_{name}", a.shape, mybir.dt.from_np(a.dtype), kind="ExternalInput").ap()
    d["x2"] = nc.dram_tensor("x2_scratch", (SEQ, D), F32, kind="Internal").ap()
    out = nc.dram_tensor("out_y", (SEQ, D), F32, kind="ExternalOutput").ap()
    build(nc, d, out)
    r = run_bass_kernel_spmd(nc, [{f"in_{name}": a for name, a in arrays.items()}], core_ids=[0])
    return r.results[0]["out_y"].reshape(1, SEQ, D)
```
